# Optimizing a Trainium2 kernel written in Bass

```python
import math
import jax, jax.numpy as jnp
from jax import lax
import numpy as np

D_MODEL = 1024
BATCH = 1
SEQ = 128
DEPTH = 2
DEC_BATCH = 1
DEC_SEQ = 128
PAST_LEN = 128

GRID_W = 64
N_EVEN = (DEPTH + 1) // 2
N_ODD = DEPTH // 2
A_W = D_MODEL // 2
DH_A = 64
H_A = A_W // DH_A
NA_KH = 8
NA_KW = 16
QCB = 16
KCB = 32
NCB = GRID_W // QCB
B_W = D_MODEL // 2
DK = 128
DV = 128
H_B = B_W // DK
CONV_K = 3
CHUNK = 64
MIX_W = A_W + B_W
IN_COLS = 3 * A_W + 4 * B_W + 4 * H_B
POOL_WINDOWS = (2, 4, 8, 16)
POOL_G = D_MODEL // len(POOL_WINDOWS)
D_FF = 7 * D_MODEL // 2
N_EXP = 8
TOP_K = 2
EPS = 1e-6
NEG_INF = -1e30

kernel_name = 'hybrid_diffusion_prefix_step'

def _rmsnorm(x, g):
    xf = x.astype(jnp.float32)
    y = xf * lax.rsqrt(jnp.mean(xf * xf, axis=-1, keepdims=True) + EPS)
    return y.astype(x.dtype) * g

def _l2norm(x):
    xf = x.astype(jnp.float32)
    return (xf * lax.rsqrt(jnp.sum(xf * xf, axis=-1, keepdims=True) + EPS)).astype(x.dtype)

def _adaln(cond, w, b):
    m = jax.nn.silu(cond) @ w + b
    return [t[:, None, :] for t in jnp.split(m, 6, axis=-1)]

def _modulate(x, g, shift, scale):
    return _rmsnorm(x, g) * (1 + scale) + shift

def _dwconv_centred(x, w):
    T = x.shape[1]
    left = (CONV_K - 1) // 2
    xp = jnp.pad(x, ((0, 0), (left, CONV_K - 1 - left), (0, 0)))
    y = xp[:, 0:T] * w[0]
    for i in range(1, CONV_K):
        y = y + xp[:, i:i + T] * w[i]
    return y

def _even_project(h, w_in, conv_w, a_log, dt_bias):
    bsz, T, _ = h.shape
    proj = h @ w_in
    a_qkv, b_qkv, b_z, b_ab = jnp.split(proj, [3 * A_W, 3 * A_W + 3 * B_W, 3 * A_W + 4 * B_W], axis=-1)
    qa, ka, va = [t.reshape(bsz, T, H_A, DH_A) for t in jnp.split(a_qkv, 3, axis=-1)]
    b_qkv = jax.nn.silu(_dwconv_centred(b_qkv, conv_w))
    qb, kb, vb = jnp.split(b_qkv, 3, axis=-1)
    qb = _l2norm(qb.reshape(bsz, T, H_B, DK))
    kb = _l2norm(kb.reshape(bsz, T, H_B, DK))
    vb = vb.reshape(bsz, T, H_B, DV)
    z = b_z.reshape(bsz, T, H_B, DV)
    ab = b_ab.astype(jnp.float32).reshape(bsz, T, 2, 2, H_B)
    g = -jnp.exp(a_log.astype(jnp.float32)) * jax.nn.softplus(ab[:, :, 0] + dt_bias.astype(jnp.float32))
    beta = jax.nn.sigmoid(ab[:, :, 1])
    return qa, ka, va, qb, kb, vb, z, g, beta

def _delta_chunked(q, k, v, g, beta, s0):
    bsz, T, H, _ = q.shape
    dv = v.shape[-1]
    n = T // CHUNK

    def chunks(a):
        a = a.astype(jnp.float32).reshape((bsz, n, CHUNK, H) + a.shape[3:])
        return jnp.moveaxis(a, (1, 3), (0, 2))

    q = chunks(q) * (DK ** -0.5)
    k, v, g, beta = chunks(k), chunks(v), chunks(g), chunks(beta)
    gc = jnp.cumsum(g, axis=-1)
    kb = k * beta[..., None]
    vb = v * beta[..., None]
    lower = jnp.tril(jnp.ones((CHUNK, CHUNK), bool))
    strict = jnp.tril(jnp.ones((CHUNK, CHUNK), bool), -1)
    diff = gc[..., :, None] - gc[..., None, :]
    decay = jnp.where(lower, jnp.exp(jnp.where(lower, diff, 0.0)), 0.0)
    lmat = jnp.where(strict, jnp.einsum('nbhid,nbhjd->nbhij', kb, k) * decay, 0.0)
    eye = jnp.eye(CHUNK, dtype=jnp.float32)
    tinv = lax.linalg.triangular_solve(eye + lmat, jnp.broadcast_to(eye, lmat.shape), left_side=True, lower=True)
    u = tinv @ vb
    w = tinv @ (kb * jnp.exp(gc)[..., None])
    attn = jnp.einsum('nbhid,nbhjd->nbhij', q, k) * decay
    qg = q * jnp.exp(gc)[..., None]
    kd = k * jnp.exp(gc[..., -1:] - gc)[..., None]
    gl = jnp.exp(gc[..., -1])[..., None, None]

    def step(S, xs):
        u_i, w_i, qg_i, a_i, kd_i, gl_i = xs
        v_new = u_i - w_i @ S
        o_i = qg_i @ S + a_i @ v_new
        S = S * gl_i + jnp.swapaxes(kd_i, -1, -2) @ v_new
        return S, o_i

    s_fin, o = lax.scan(step, s0.astype(jnp.float32), (u, w, qg, attn, kd, gl))
    o = jnp.moveaxis(o, (0, 2), (1, 3)).reshape(bsz, T, H, dv)
    return o, s_fin

def _delta_bidir(q, k, v, g, beta, s0):
    o_f, s_f = _delta_chunked(q, k, v, g[:, :, 0], beta[:, :, 0], s0[:, 0])
    flip = lambda a: jnp.flip(a, axis=1)
    o_b, s_b = _delta_chunked(flip(q), flip(k), flip(v), flip(g[:, :, 1]), flip(beta[:, :, 1]), s0[:, 1])
    return (o_f + flip(o_b)).astype(v.dtype), jnp.stack([s_f, s_b], axis=1)

def _even_output(oa, ob, z, o_gain, w_out):
    bsz, T = oa.shape[:2]
    obf = ob.astype(jnp.float32)
    yb = obf * lax.rsqrt(jnp.mean(obf * obf, axis=-1, keepdims=True) + EPS) * o_gain * jax.nn.silu(z.astype(jnp.float32))
    y = jnp.concatenate([oa.reshape(bsz, T, A_W), yb.astype(oa.dtype).reshape(bsz, T, B_W)], axis=-1)
    return y @ w_out

def _ctx_attention(q, k, v):
    s = jnp.einsum('bqhd,bkhd->bhqk', q, k).astype(jnp.float32) * (q.shape[-1] ** -0.5)
    p = jax.nn.softmax(s, axis=-1).astype(v.dtype)
    return jnp.einsum('bhqk,bkhd->bqhd', p, v)

def _na_latent_attention(q, k, v, k_ctx, v_ctx, rpb):
    bsz, N, H, dh = q.shape
    rows = N // GRID_W
    kh = min(NA_KH, rows)
    r = np.arange(rows)
    row_idx = np.clip(r - kh // 2, 0, rows - kh)[:, None] + np.arange(kh)[None, :]
    qcol = np.arange(GRID_W).reshape(NCB, QCB)
    col_lo = np.clip(qcol - NA_KW // 2, 0, GRID_W - NA_KW)
    col_idx = np.minimum(col_lo[:, 0], GRID_W - KCB)[:, None] + np.arange(KCB)[None, :]
    kc = col_idx[:, None, :]
    valid = (kc >= col_lo[..., None]) & (kc < col_lo[..., None] + NA_KW)
    dr = row_idx - r[:, None] + (NA_KH - 1)
    dc = np.clip(kc - qcol[..., None], 1 - NA_KW, NA_KW - 1) + (NA_KW - 1)
    bias = rpb[:, dr[:, None, None, :, None], dc[None, :, :, None, :]].astype(jnp.float32)
    bias = jnp.where(valid[None, None, :, :, None, :], bias, NEG_INF)
    ri = row_idx[:, None, :, None]
    ci = col_idx[None, :, None, :]
    k_loc = k.reshape(bsz, rows, GRID_W, H, dh)[:, ri, ci]
    v_loc = v.reshape(bsz, rows, GRID_W, H, dh)[:, ri, ci]
    qb = q.reshape(bsz, rows, NCB, QCB, H, dh)
    scale = dh ** -0.5
    s_loc = jnp.einsum('brcqhd,brcjmhd->bhrcqjm', qb, k_loc).astype(jnp.float32) * scale + bias[None]
    s_ctx = jnp.einsum('brcqhd,blhd->bhrcql', qb, k_ctx).astype(jnp.float32) * scale
    n_loc = kh * KCB
    logits = jnp.concatenate([s_loc.reshape(s_loc.shape[:5] + (n_loc,)), s_ctx], axis=-1)
    p = jax.nn.softmax(logits, axis=-1).astype(v.dtype)
    p_loc = p[..., :n_loc].reshape(s_loc.shape)
    p_ctx = p[..., n_loc:]
    o = (jnp.einsum('bhrcqjm,brcjmhd->brcqhd', p_loc, v_loc)
         + jnp.einsum('bhrcql,blhd->brcqhd', p_ctx, v_ctx))
    return o.reshape(bsz, N, H, dh)

def _pool_mixer(h, pool_w, pool_scale):
    T = h.shape[1]
    hf = h.astype(jnp.float32)
    csum = jnp.pad(jnp.cumsum(hf, axis=1), ((0, 0), (1, 0), (0, 0)))
    t = np.arange(T)
    outs = []
    for gi, w in enumerate(POOL_WINDOWS):
        lo = np.maximum(t - w // 2, 0).astype(np.int32)
        hi = np.minimum(t + (w - w // 2), T).astype(np.int32)
        sl = slice(gi * POOL_G, (gi + 1) * POOL_G)
        s = csum[:, hi, sl] - csum[:, lo, sl]
        cnt = (hi - lo).astype(np.float32)[None, :, None]
        y = (s / cnt - hf[:, :, sl]).astype(h.dtype)
        outs.append(y @ pool_w[gi])
    return jnp.concatenate(outs, axis=-1) * pool_scale

def _swiglu(h, wg, wu, wd):
    return (jax.nn.silu(h @ wg) * (h @ wu)) @ wd

def _moe_swiglu(h, w_router, w_gate, w_up, w_down):
    logits = (h @ w_router).astype(jnp.float32)
    top_v, top_i = lax.top_k(logits, TOP_K)
    top_w = jax.nn.softmax(top_v, axis=-1)
    gates = jnp.sum(jax.nn.one_hot(top_i, N_EXP, dtype=jnp.float32) * top_w[..., None], axis=-2).astype(h.dtype)
    out = jnp.zeros_like(h)
    for e in range(N_EXP):
        out = out + gates[..., e:e + 1] * _swiglu(h, w_gate[e], w_up[e], w_down[e])
    return out

def _channel_mixer(h, l, ffn_gate, ffn_up, ffn_down, w_router, moe_gate, moe_up, moe_down):
    i = l // 2
    if l % 2 == 0:
        return _swiglu(h, ffn_gate[i], ffn_up[i], ffn_down[i])
    return _moe_swiglu(h, w_router[i], moe_gate[i], moe_up[i], moe_down[i])

def setup_inputs(seed: int = 0) -> dict:
    key = jax.random.key(seed)
    keys = iter(jax.random.split(key, 40))

    def nrm(shape, scale):
        return jax.random.normal(next(keys), shape, jnp.float32) * scale

    d = D_MODEL
    dt = jnp.exp(jax.random.uniform(next(keys), (N_EVEN, 2, H_B), jnp.float32, math.log(1e-3), math.log(1e-1)))
    a_log = jnp.log(jax.random.uniform(next(keys), (N_EVEN, 2, H_B), jnp.float32, 1.0, 16.0))
    return {
        'x_prompt': nrm((BATCH, SEQ, d), 1.0),
        'x_sample': nrm((DEC_BATCH, DEC_SEQ, d), 1.0),
        'cache_k_ctx': nrm((DEC_BATCH, N_EVEN, PAST_LEN, H_A, DH_A), 1.0),
        'cache_v_ctx': nrm((DEC_BATCH, N_EVEN, PAST_LEN, H_A, DH_A), 1.0),
        'state_delta': nrm((DEC_BATCH, N_EVEN, 2, H_B, DK, DV), 0.1),
        'c': nrm((DEC_BATCH, d), 1.0),
        'c_ctx': nrm((d,), 1.0),
        'w_mod': nrm((DEPTH, d, 6 * d), 0.5 * d ** -0.5),
        'b_mod': nrm((DEPTH, 6 * d), 0.02),
        'norm_g': 1.0 + nrm((DEPTH, 2, d), 0.1),
        'final_g': 1.0 + nrm((d,), 0.1),
        'w_in': nrm((N_EVEN, d, IN_COLS), d ** -0.5),
        'conv_w': nrm((N_EVEN, CONV_K, 3 * B_W), CONV_K ** -0.5),
        'a_log': a_log,
        'dt_bias': dt + jnp.log(-jnp.expm1(-dt)),
        'rpb': nrm((N_EVEN, H_A, 2 * NA_KH - 1, 2 * NA_KW - 1), 0.1),
        'o_gain': 1.0 + nrm((N_EVEN, DV), 0.1),
        'w_out': nrm((N_EVEN, MIX_W, d), MIX_W ** -0.5),
        'ffn_gate': nrm((N_EVEN, d, D_FF), d ** -0.5),
        'ffn_up': nrm((N_EVEN, d, D_FF), d ** -0.5),
        'ffn_down': nrm((N_EVEN, D_FF, d), D_FF ** -0.5),
        'pool_w': nrm((N_ODD, len(POOL_WINDOWS), POOL_G, POOL_G), POOL_G ** -0.5),
        'pool_scale': 1.0 + nrm((N_ODD, d), 0.1),
        'w_router': nrm((N_ODD, d, N_EXP), d ** -0.5),
        'moe_gate': nrm((N_ODD, N_EXP, d, D_FF), d ** -0.5),
        'moe_up': nrm((N_ODD, N_EXP, d, D_FF), d ** -0.5),
        'moe_down': nrm((N_ODD, N_EXP, D_FF, d), D_FF ** -0.5),
    }

def reference(x_prompt, x_sample, cache_k_ctx, cache_v_ctx, state_delta, c, c_ctx,
              w_mod, b_mod, norm_g, final_g, w_in, conv_w, a_log, dt_bias, rpb, o_gain, w_out,
              ffn_gate, ffn_up, ffn_down, pool_w, pool_scale, w_router, moe_gate, moe_up, moe_down):
    x = x_prompt
    k_list, v_list, s_list = [], [], []
    for l in range(DEPTH):
        sh1, sc1, gt1, sh2, sc2, gt2 = _adaln(c_ctx[None, :], w_mod[l], b_mod[l])
        h = _modulate(x, norm_g[l, 0], sh1, sc1)
        if l % 2 == 0:
            i = l // 2
            qa, ka, va, qb, kb, vb, z, g, beta = _even_project(h, w_in[i], conv_w[i], a_log[i], dt_bias[i])
            oa = _ctx_attention(qa, ka, va)
            s0 = jnp.zeros((x.shape[0], 2, H_B, DK, DV), jnp.float32)
            ob, s_fin = _delta_bidir(qb, kb, vb, g, beta, s0)
            mix = _even_output(oa, ob, z, o_gain[i], w_out[i])
            k_list.append(ka)
            v_list.append(va)
            s_list.append(s_fin.astype(x.dtype))
        else:
            mix = _pool_mixer(h, pool_w[l // 2], pool_scale[l // 2])
        x = x + gt1 * mix
        h = _modulate(x, norm_g[l, 1], sh2, sc2)
        x = x + gt2 * _channel_mixer(h, l, ffn_gate, ffn_up, ffn_down, w_router, moe_gate, moe_up, moe_down)
    y_prompt = _rmsnorm(x, final_g)
    new_k_ctx = jnp.stack(k_list, axis=1)
    new_v_ctx = jnp.stack(v_list, axis=1)
    new_state_delta = jnp.stack(s_list, axis=1)

    x = x_sample
    for l in range(DEPTH):
        sh1, sc1, gt1, sh2, sc2, gt2 = _adaln(c, w_mod[l], b_mod[l])
        h = _modulate(x, norm_g[l, 0], sh1, sc1)
        if l % 2 == 0:
            i = l // 2
            qa, ka, va, qb, kb, vb, z, g, beta = _even_project(h, w_in[i], conv_w[i], a_log[i], dt_bias[i])
            oa = _na_latent_attention(qa, ka, va, cache_k_ctx[:, i], cache_v_ctx[:, i], rpb[i])
            ob, _ = _delta_bidir(qb, kb, vb, g, beta, state_delta[:, i])
            mix = _even_output(oa, ob, z, o_gain[i], w_out[i])
        else:
            mix = _pool_mixer(h, pool_w[l // 2], pool_scale[l // 2])
        x = x + gt1 * mix
        h = _modulate(x, norm_g[l, 1], sh2, sc2)
        x = x + gt2 * _channel_mixer(h, l, ffn_gate, ffn_up, ffn_down, w_router, moe_gate, moe_up, moe_down)
    y_sample = _rmsnorm(x, final_g)
    return (y_prompt, y_sample, new_k_ctx, new_v_ctx, new_state_delta)


_drawn_inputs = setup_inputs


def setup_inputs(seed=0):
    import zlib

    import numpy as np

    out = dict(_drawn_inputs(seed))
    spreads = {}
    factors = {'rpb': 32.299, 'o_gain': 3.639, 'cache_k_ctx': 3.035}
    for name, (base, spread) in spreads.items():
        noise = np.random.default_rng([zlib.crc32(name.encode()), seed]).standard_normal(out[name].shape)
        drawn = base * np.exp(spread * noise) if base else spread * noise
        out[name] = __import__('jax').numpy.asarray(drawn.astype(out[name].dtype))
    for name, factor in factors.items():
        out[name] = (out[name] * factor).astype(out[name].dtype)
    return out
```

```python
from contextlib import ExitStack

import concourse.bass as bass
from concourse import mybir

F32 = mybir.dt.float32
R32 = mybir.dt.float32r
I32 = mybir.dt.int32
U32 = mybir.dt.uint32
BF16 = mybir.dt.bfloat16
ALU = mybir.AluOpType
ACT = mybir.ActivationFunctionType
AX = mybir.AxisListType

P = 128
D = 1024
KT = D // P
NB = 2
H_A, DH_A, A_W = 8, 64, 512
H_B, DK, B_W = 4, 128, 512
GRID_W = 64
NA_KW = 16
NROW = P // GRID_W
CONV_K = 3
D_FF = 3584
NC = D_FF // 512
N_EXP = 8
POOL_WINDOWS = (2, 4, 8, 16)
POOL_G = 256
EPS = 1e-6
NEG = -1e30
RAW = 6
SPLIT = 3
LEVELS = 7

MOD0 = 0
WIN = MOD0 + 24
MOD1 = WIN + 14
WOUT = MOD1 + 24
FFN = WOUT + 4
MOE = FFN + 6 * NC
UNITS_E = 6 * NC
assert FFN % RAW == 0 and MOE % RAW == 0 and UNITS_E % RAW == 0

WIN_ORDER = (("b", 3), ("b", 4), ("b", 5), ("aq", 0), ("ak", 1), ("av", 2), ("z", 6))

SEMS = """LT_saved L_beta L_masked L_turned ab_saved ab_turned acc_added acc_zeroed act_step attnT_saved
attn_masked attn_turned band_ready band_scaled beta_ready bias_loaded bias_masked cache_loaded
cols_saved consts_ready conv_done conv_mid conv_sum counts_turned csil_ready csplit_ready ct_ready
decay_ready diag_ready diff_ready dve_step egc_ready finalg_loaded g_ready gates_saved gates_turned
gathered_hi gathered_lo gc_saved gc_turned gcol_ready gcrow_turned grep_ready hT_by_scalar
hT_by_vector h_hi_ready h_lo_ready h_ready h_turned hc_hi hc_lo hi_ready htok_hi htok_lo
htok_turned k_saved k_turned kd_ready kdf_ready kn_ready ks_turned ktok_saved ktok_turned lo_ready
logits_turned m1_saved m1_turned mask_ready mod_cols_saved mod_cols_turned mod_rows_copied mx_ready
npass_ready o_b_turned o_turned oa_ready ob0_ready pT_saved p_exp p_in p_turned pool_mixed
pool_step pooled poolw_loaded pos_turned proj_saved qn_ready qs_turned result_zeroed rhs_ready
route_dd route_exp rows_loaded rows_turned rq_ready s_saved scattered scores_turned scp_ready
silu_ready silu_z small_loaded soft_in softplus_l sq_ready ss_turned st_ready state_saved
state_stored state_turned std_ready sumsq_ready tri_ready v_turned var_ready vnew_saved vnew_turned
weights_used x1_tmp x_loaded x_updated xg_hi xg_lo xn_ready xn_turned xx_saved xx_turned yT_hi
yT_lo y_hi y_lo y_ready y_stored y_turned yb_ready yp_ready yss_ready ystd_ready z_gained zr_ready""".split()


def rep(ap, axis, n):
    shape = list(ap.shape)
    shape.insert(axis, n)
    return ap.unsqueeze(axis).broadcast_to(shape)


def build(nc, x_prompt, x_sample, cache_k, cache_v, state0, c, c_ctx, w_mod, b_mod, norm_g, final_g,
          w_in, conv_w, a_log, dt_bias, rpb, o_gain, w_out, ffn_gate, ffn_up, ffn_down, pool_w,
          pool_scale, w_router, moe_gate, moe_up, moe_down,
          y_prompt, y_sample, new_k, new_v, new_state):
    top = ExitStack()
    with top:
        def sbuf(stack, name, shape, dt=F32):
            return stack.enter_context(nc.sbuf_tensor(name, [P, *shape], dt))

        s = {n: top.enter_context(nc.semaphore(n)) for n in SEMS}
        raw_full = [top.enter_context(nc.semaphore(f"raw_full{i}")) for i in range(RAW)]
        ps = top.enter_context(nc.psum_tensor("ps", [P, 8, 512], F32))

        raw = sbuf(top, "raw", [RAW, 4, 512])
        w_hi = sbuf(top, "w_hi", [SPLIT, 4, 512], R32)
        w_lo = sbuf(top, "w_lo", [SPLIT, 4, 512], R32)
        x = sbuf(top, "x", [NB, D])
        ident = sbuf(top, "ident", [P])
        ones = sbuf(top, "ones", [P])
        eps = sbuf(top, "eps", [1])
        fold = sbuf(top, "fold", [2])
        rowsA = sbuf(top, "rowsA", [P])
        rowsB = sbuf(top, "rowsB", [P])
        cols = sbuf(top, "cols", [92])
        bcol = sbuf(top, "bcol", [2, 48])
        mcol = sbuf(top, "mcol", [2, 48, NB])
        scp = sbuf(top, "scp", [4, KT, NB])
        gcol = sbuf(top, "gcol", [4, KT, NB])
        sumsq = sbuf(top, "sumsq", [NB])
        var = sbuf(top, "var", [NB])
        std = sbuf(top, "std", [NB])
        rstd = sbuf(top, "rstd", [NB])
        c_cols = cols[:, 0:16]
        ng_cols = cols[:, 16:48].rearrange("p (w k) -> p w k", k=KT)
        conv_cols = cols[:, 48:84].rearrange("p (i t) -> p i t", i=CONV_K)
        pscale_cols = cols[:, 84:92]

        mixer = ExitStack()
        tri = sbuf(mixer, "tri", [4, P])
        lev = sbuf(mixer, "lev", [LEVELS, 2, P], BF16)
        b_ch = sbuf(mixer, "b_ch", [12, 256])
        R = sbuf(mixer, "R", [16, P])
        qTA = R[:, 0:8].rearrange("p (a c) n -> p a (c n)", c=2)
        kTA = R[:, 8:16].rearrange("p (a c) n -> p a (c n)", c=2)
        vA = sbuf(mixer, "vA", [NB, 512])
        z = sbuf(mixer, "z", [NB, 512])
        y = sbuf(mixer, "y", [NB, D])
        bias = sbuf(mixer, "bias", [H_A, P])
        rev = sbuf(mixer, "rev", [P])
        kc = sbuf(mixer, "kc", [512])
        vc = sbuf(mixer, "vc", [512])
        kcT = sbuf(mixer, "kcT", [4, P])
        s0 = sbuf(mixer, "s0", [2, H_B, DK])
        ab = sbuf(mixer, "ab", [NB, 16])
        w_ab = sbuf(mixer, "w_ab", [KT, 16])
        sm = sbuf(mixer, "sm", [24, 16])
        ogain = sbuf(mixer, "ogain", [DK])
        alog = sbuf(mixer, "alog", [8])
        dtb = sbuf(mixer, "dtb", [8])
        front = ExitStack()
        csil = sbuf(front, "csil", [16])
        csp = sbuf(front, "csp", [KT, P], R32)
        m4 = sbuf(front, "m4", [3, 512])
        xn0 = sbuf(front, "xn0", [NB, D])
        hTf0 = sbuf(front, "hTf0", [KT, 256])
        hTh0 = sbuf(front, "hTh0", [KT, 256], R32)
        hTl0 = sbuf(front, "hTl0", [KT, 256], R32)
        front.close()
        work = ExitStack()
        T = [sbuf(work, f"T{i}", [16, P]) for i in range(7)]
        work.close()
        decay, attn, LT, CTa, X, XT, M1 = T
        mixer.close()

        tail = ExitStack()
        gate_bc = sbuf(tail, "gate_bc", [NB, D])
        diag = sbuf(tail, "diag", [4, 4, P])
        tmp = sbuf(tail, "tmp", [NB, 512])
        xn1 = sbuf(tail, "xn1", [NB, D])
        hTf1 = sbuf(tail, "hTf1", [KT, 256])
        hTh1 = sbuf(tail, "hTh1", [KT, 256], R32)
        hTl1 = sbuf(tail, "hTl1", [KT, 256], R32)
        sg = sbuf(tail, "sg", [NB, 512])
        hc = sbuf(tail, "hc", [NB, 512])
        hcTh = sbuf(tail, "hcTh", [4, 256], R32)
        hcTl = sbuf(tail, "hcTl", [4, 256], R32)
        zr = sbuf(tail, "zr", [640], R32)
        band = sbuf(tail, "band", [4, P])
        pooling = ExitStack()
        poolw = sbuf(pooling, "poolw", [KT, POOL_G])
        pooling.close()
        htok_h = sbuf(tail, "htok_h", [NB, D], R32)
        htok_l = sbuf(tail, "htok_l", [NB, D], R32)
        yh = sbuf(tail, "yh", [D], R32)
        yl = sbuf(tail, "yl", [D], R32)
        ST = sbuf(tail, "ST", [NB, P], R32)
        Sm = sbuf(tail, "Sm", [NB, P], R32)
        iota = sbuf(tail, "iota", [P])
        sup = sbuf(tail, "sup", [P])
        w_rt = sbuf(tail, "w_rt", [KT, N_EXP])
        rt = sbuf(tail, "rt", [16, NB, N_EXP])
        idx8 = sbuf(tail, "idx8", [NB, 8], U32)
        posj = sbuf(tail, "posj", [NB * N_EXP + 1, NB])
        gatej = sbuf(tail, "gatej", [NB * N_EXP + 1, NB])
        gcur = sbuf(tail, "gcur", [NB])
        npass = sbuf(tail, "npass", [1], I32)
        tail.close()
        acc = xn1
        finalg = diag[:, 0:2].rearrange("p a k n -> p (a k n)")
        block = top.enter_context(nc.Block())

        def flat(t):
            return t.rearrange("p a b -> p (a b)")

        def load(sp, n, k, src, first=False):
            if not first:
                sp.wait_ge(s["lo_ready"], n - RAW + 1)
            sp.dma_start(raw[:, k % RAW], src).then_inc(raw_full[k % RAW], 16)

        def split_hi(act, n, k, turn):
            act.wait_ge(raw_full[k % RAW], 16 * turn)
            act.wait_ge(s["weights_used"], n + 1)
            nc.scalar.activation(w_hi[:, k % SPLIT], raw[:, k % RAW], ACT.Copy).then_inc(s["hi_ready"], 1)

        def split_lo(dve, n, k):
            dve.wait_ge(s["hi_ready"], n + 1)
            nc.vector.tensor_tensor(w_lo[:, k % SPLIT], raw[:, k % RAW], w_hi[:, k % SPLIT].bitcast(F32),
                                    ALU.subtract).then_inc(s["lo_ready"], 1)

        def used(n):
            return n + 1 + SPLIT

        def rows(w, kt0, c0):
            return w.rearrange("(t p) n -> p t n", p=P)[:, kt0:kt0 + 4, bass.ds(c0, 512)]

        def multiply(pe, n, k, xh, xl, kt0, banks, start, stop):
            pe.wait_ge(s["lo_ready"], n + 1)
            for i, (b, bank) in enumerate(banks):
                cut = slice(b * P, b * P + P)
                for t in range(4):
                    st = start and t == 0
                    en = stop and t == 3
                    nc.tensor.matmul(ps[:, bank, :], xh[:, kt0 + t, cut], w_hi[:, k % SPLIT, t, :], start=st, stop=False)
                    nc.tensor.matmul(ps[:, bank, :], xl[:, kt0 + t, cut], w_hi[:, k % SPLIT, t, :], start=False, stop=False)
                    last = nc.tensor.matmul(ps[:, bank, :], xh[:, kt0 + t, cut], w_lo[:, k % SPLIT, t, :],
                                            start=False, stop=en)
            last.then_inc(s["weights_used"], 1)

        @block.sync
        def _(sp):
            def mod_load(l, base, i0):
                def body(i, first=False):
                    for k in range(6):
                        load(sp, base + 6 * i + k, base + k, rows(w_mod[l], 4 * (k % 2), (3 * i + k // 2) * 512), first)
                if i0:
                    body(0, first=True)
                with sp.Fori(i0, 4) as i:
                    body(i)

            for part, src in ((rowsA[0:8, :], c_ctx.rearrange("(k p) -> k p", p=P)),
                              (rowsA[8:16, :], c[0].rearrange("(k p) -> k p", p=P)),
                              (rowsA[16:48, :], norm_g.rearrange("l w (k p) -> (l w k) p", p=P)),
                              (rowsA[48:84, :], conv_w[0].rearrange("i (t p) -> (i t) p", p=P)),
                              (rowsA[84:92, :], pool_scale[0].rearrange("(k p) -> k p", p=P)),
                              (rowsB[0:96, :], b_mod.rearrange("l (k p) -> (l k) p", p=P))):
                sp.dma_start(part, src).then_inc(s["rows_loaded"], 16)
            mod_load(0, MOD0, 1)
            for i, (_, ch) in enumerate(WIN_ORDER):
                for h in range(2):
                    n = WIN + 2 * i + h
                    load(sp, n, n, rows(w_in[0], 4 * h, ch * 512))
            mod_load(1, MOD1, 0)
            for n in range(WOUT, FFN):
                load(sp, n, n, rows(w_out[0], 4 * ((n - WOUT) % 2), (n - WOUT) // 2 * 512))

            def swiglu(n0, gate, up, down):
                for k in range(4):
                    load(sp, n0 + k, k, rows(gate if k < 2 else up, 4 * (k % 2), 0))
                with sp.Fori(1, NC) as cc:
                    m = n0 + 6 * cc - 2
                    for k in range(6):
                        src = (rows(gate if k < 2 else up, 4 * (k % 2), cc * 512) if k < 4 else
                               down.rearrange("(c t p) n -> c p t n", p=P, t=4)[
                                   cc - 1, :, :, (k - 4) * 512:(k - 3) * 512])
                        load(sp, m + k, 4 + k, src)
                for k in range(2):
                    load(sp, n0 + UNITS_E - 2 + k, 4 + k,
                         down.rearrange("(c t p) n -> c p t n", p=P, t=4)[NC - 1, :, :, k * 512:(k + 1) * 512])

            swiglu(FFN, ffn_gate[0], ffn_up[0], ffn_down[0])
            with sp.Fori(0, N_EXP) as e:
                swiglu(MOE + UNITS_E * e, moe_gate[0, e], moe_up[0, e], moe_down[0, e])
            sp.wait_ge(s["npass_ready"], 1)
            passes = nc.sync.value_load(npass[0:1, 0:1], min_val=1, max_val=2)
            with sp.If(passes > 1):
                with sp.Fori(0, N_EXP) as e:
                    swiglu(MOE + UNITS_E * N_EXP + UNITS_E * e, moe_gate[0, e], moe_up[0, e], moe_down[0, e])
            sp.wait_ge(s["y_ready"], 1)
            sp.dma_start(y_prompt[0], xn1[:, 0]).then_inc(s["y_stored"], 16)
            sp.dma_start(y_sample[0], xn1[:, 1]).then_inc(s["y_stored"], 16)
            sp.wait_ge(s["y_stored"], 32)
            sp.wait_ge(s["state_stored"], 48)

        @block.gpsimd
        def _(pool):
            steps = [0]

            def step(ins):
                steps[0] += 1
                ins.then_inc(s["pool_step"], 1)
                pool.wait_ge(s["pool_step"], steps[0])

            def keep(ap, pattern, base, mult, fill=0.0, op=ALU.is_ge):
                step(nc.gpsimd.affine_select(out=ap, in_=ap, compare_op=op, fill=fill, base=base,
                                             pattern=pattern, channel_multiplier=mult))

            step(nc.gpsimd.memset(ident[:, :], 0.0))
            keep(ident[:, :], [[-1, P]], 0, 1, fill=1.0, op=ALU.not_equal)
            step(nc.gpsimd.memset(ones[:, :], 1.0))
            step(nc.gpsimd.memset(eps[:, :], EPS))
            nc.gpsimd.tensor_tensor(fold[:, :], ident[:, 0:2], ident[:, 2:4], ALU.add).then_inc(s["consts_ready"], 1)
            step(nc.gpsimd.memset(tri[:, :, :], 1.0))
            keep(tri[:, 0], [[-1, P]], 0, 1)
            keep(tri[:, 1], [[1, P]], 0, -1)
            keep(tri[:, 2], [[-1, P]], -1, 1)
            keep(tri[:, 3], [[1, P]], -1, -1)
            pool.sem_inc(s["tri_ready"], 1)
            step(nc.gpsimd.memset(rev[:, :], 0.0))
            for r in range(NROW):
                cut = slice(r * GRID_W, (r + 1) * GRID_W)
                keep(rev[cut, cut], [[1, GRID_W]], 1 - GRID_W, 1, fill=1.0, op=ALU.not_equal)
            step(nc.gpsimd.memset(lev[:, :, :, :], 0.0))
            for l in range(LEVELS):
                h = 1 << l
                v = lev[:, l].rearrange("p d (b r) -> p d b r", r=2 * h)
                n = P // (2 * h)
                step(nc.gpsimd.memset(v[:, 0, :, h:], 1.0))
                keep(v[:, 0, :, h:], [[-2 * h, n], [0, h]], 0, 1)
                keep(v[:, 0, :, h:], [[2 * h, n], [0, h]], h - 1, -1)
                step(nc.gpsimd.memset(v[:, 1, :, 0:h], 1.0))
                keep(v[:, 1, :, 0:h], [[-2 * h, n], [0, h]], -h, 1)
                keep(v[:, 1, :, 0:h], [[2 * h, n], [0, h]], 2 * h - 1, -1)
            pool.wait_ge(s["bias_loaded"], 64)
            for r in range(NROW):
                v = bias[r * GRID_W:(r + 1) * GRID_W].rearrange("p h (r c) -> p (h r) c", r=NROW)
                hi = GRID_W - NA_KW
                keep(v[:, :, 0:hi], [[0, H_A * NROW], [1, hi]], NA_KW // 2 - GRID_W + 1, 1, fill=NEG)
                keep(v[:, :, NA_KW:], [[0, H_A * NROW], [-1, hi]], GRID_W - 1 + NA_KW // 2 - 1 - NA_KW, -1, fill=NEG)
            pool.sem_inc(s["bias_masked"], 1)

            pool.wait_ge(s["g_ready"], 1)
            pool.wait_ge(s["mod_cols_saved"], 9)
            nc.gpsimd.tensor_copy(attn[:, :, :], rep(sm[:, 8], 2, P)).then_inc(s["grep_ready"], 1)
            pool.wait_ge(s["silu_z"], 1)
            nc.gpsimd.tensor_tensor(z.rearrange("p b (h v) -> p (b h) v", v=DK), z.rearrange("p b (h v) -> p (b h) v", v=DK),
                                    rep(ogain[:, :], 1, 8), ALU.mult).then_inc(s["z_gained"], 1)
            for b in range(NB):
                pool.wait_ge(s["L_beta"], b + 1)
                for t, m, name in ((decay, 2, "L_masked"), (attn, 0, "attn_masked")):
                    v = t[:, 8 * b:8 * b + 8].rearrange("p (d h) n -> p d h n", d=2)
                    nc.gpsimd.tensor_tensor(v, v, rep(tri[:, m:m + 2], 2, H_B), ALU.mult).then_inc(s[name], 1)
            pool.wait_ge(s["oa_ready"], 2)
            for g in range(4):
                cut = slice(4 * g, 4 * g + 4)
                if g % 2 == 0:
                    pool.wait_ge(s["L_masked"], g // 2 + 1)
                nc.gpsimd.tensor_tensor(X[:, cut], decay[:, cut], rep(lev[:, 0, 1 - g % 2], 1, 4), ALU.mult)\
                    .then_inc(s["x1_tmp"], 1)
            pool.wait_ge(s["LT_saved"], 1)
            for g in range(4):
                cut = slice(4 * g, 4 * g + 4)
                nc.gpsimd.tensor_tensor(XT[:, cut], LT[:, cut], rep(lev[:, 0, g % 2], 1, 4), ALU.mult)\
                    .then_inc(s["x1_tmp"], 1)
            for l in range(1, LEVELS):
                ct = (CTa, decay)[(l - 1) % 2]
                if l == 2:
                    pool.wait_ge(s["L_turned"], 1)
                    pool.wait_ge(s["x1_tmp"], 8)
                if l >= 3:
                    pool.wait_ge(s["m1_turned"], 4 * (l - 2))
                for b in range(NB):
                    nc.gpsimd.tensor_tensor(ct[:, 8 * b:8 * b + 8].rearrange("p (d h) n -> p d h n", d=2),
                                            LT[:, 8 * b:8 * b + 8].rearrange("p (d h) n -> p d h n", d=2),
                                            rep(lev[:, l], 2, H_B), ALU.mult).then_inc(s["ct_ready"], 1)
            pool.wait_ge(s["m1_turned"], 20)
            pool.wait_ge(s["kdf_ready"], 1)
            pool.wait_ge(s["ktok_saved"], 1)
            for d in range(2):
                nc.gpsimd.tensor_tensor(CTa[:, 4 * d:4 * d + 4], b_ch[:, 8:10].rearrange("p a (c n) -> p (a c) n", n=P),
                                        rep(sm[:, 13, 4 * d:4 * d + 4], 2, P), ALU.mult).then_inc(s["kd_ready"], 1)

            pool.wait_ge(s["y_turned"], 2)
            pool.wait_ge(s["state_stored"], 48)
            nc.gpsimd.memset(zr[:, :].bitcast(F32), 0.0).then_inc(s["zr_ready"], 1)

            def gates(i):
                pool.wait_ge(s["gcol_ready"], i // 2 + 1)
                if i:
                    pool.wait_ge(s["gates_turned"], i)
                for b in range(NB):
                    for h in range(2):
                        nc.gpsimd.tensor_tensor(diag[:, 2 * b + h], rep(ident[:, :], 1, 4),
                                                rep(gcol[:, i, 4 * h:4 * h + 4, b], 2, P), ALU.mult)\
                            .then_inc(s["diag_ready"], 1)

            gates(0)
            gates(1)
            step(nc.gpsimd.memset(band[:, :, :], 1.0))
            for i, w in enumerate(POOL_WINDOWS):
                keep(band[:, i], [[-1, P]], w // 2, 1)
                keep(band[:, i], [[1, P]], w - w // 2 - 1, -1)
            step(nc.gpsimd.memset(sup[:, :], 1.0))
            keep(sup[:, :], [[1, P]], -1, -1)
            step(nc.gpsimd.memset(posj[:, :, :], -1.0))
            step(nc.gpsimd.memset(gatej[:, :, :], 0.0))
            nc.gpsimd.iota(iota[:, :], pattern=[[1, P]], base=0, channel_multiplier=0,
                           allow_small_or_imprecise_dtypes=True).then_inc(s["band_ready"], 1)
            gates(2)
            gates(3)
            pool.wait_ge(s["xn_turned"], 6)
            nc.gpsimd.memset(Sm[:, :, :].bitcast(F32), 0.0)
            nc.gpsimd.memset(gcur[:, :], 0.0)
            nc.gpsimd.memset(acc[:, :, :], 0.0).then_inc(s["acc_zeroed"], 1)

        @block.scalar
        def _(act):
            steps = [0]

            def step(ins):
                steps[0] += 1
                ins.then_inc(s["act_step"], 1)
                act.wait_ge(s["act_step"], steps[0])

            def fetch(dst, src, name):
                act.dma_start(dst, src).then_inc(s[name], 16)

            act.wait_ge(s["rows_loaded"], 96)
            fetch(x[:, 0], x_prompt[0], "x_loaded")
            fetch(x[:, 1], x_sample[0], "x_loaded")
            fetch(w_ab[:, :, :], w_in[0].rearrange("(t p) n -> p t n", p=P)[:, :, 7 * 512:7 * 512 + 16], "small_loaded")
            fetch(alog[:, :], a_log[0].rearrange("d h -> (d h)").partition_broadcast(P), "small_loaded")
            fetch(dtb[:, :], dt_bias[0].rearrange("d h -> (d h)").partition_broadcast(P), "small_loaded")
            fetch(ogain[:, :], o_gain[0].partition_broadcast(P), "small_loaded")
            fetch(s0[:, :, :, :], state0[0, 0].rearrange("d h k v -> k d h v"), "cache_loaded")
            fetch(kc[:, :], cache_k[0, 0].rearrange("t h d -> t (h d)"), "cache_loaded")
            fetch(vc[:, :], cache_v[0, 0].rearrange("t h d -> t (h d)"), "cache_loaded")
            nh, nr, nd = rpb.shape[1:]
            for qr in range(NROW):
                for kr in range(NROW):
                    src = bass.AP(tensor=rpb.tensor, offset=(nr // 2 + kr - qr) * nd + nd // 2 - (GRID_W - 1),
                                  ap=[[1, GRID_W], [nr * nd, nh], [1, GRID_W]])
                    fetch(bias[qr * GRID_W:(qr + 1) * GRID_W, :, kr * GRID_W:(kr + 1) * GRID_W], src, "bias_loaded")

            act.wait_ge(s["rows_turned"], 1)
            nc.scalar.activation(csil[:, :], ps[:, 7, 0:16], ACT.Silu).then_inc(s["csil_ready"], 1)

            def mod_split(base, l):
                with act.Fori(0, 4) as i:
                    def copy_row(j):
                        act.wait_ge(s["weights_used"], used(base + 6 * i + 2 * j + 1))
                        nc.scalar.activation(m4[0:4, j], ps[0:4, j, :], ACT.Copy).then_inc(s["mod_rows_copied"], 1)
                    for j in range(3):
                        for h in range(2):
                            k = base + 2 * j + h
                            split_hi(act, base + 6 * i + 2 * j + h, k, k // RAW + 1 + i)
                        if j:
                            copy_row(j - 1)
                    copy_row(2)

            def norm(i):
                xn = xn0 if i == 0 else xn1
                if i == 0:
                    act.wait_ge(s["x_loaded"], 32)
                else:
                    act.wait_ge(s["x_updated"], i)
                for b in range(NB):
                    nc.scalar.activation(xn[:, b], x[:, b], ACT.Square, accum_out=sumsq[:, b:b + 1])\
                        .then_inc(s["sumsq_ready"], 1)
                act.wait_ge(s["var_ready"], i + 1)
                nc.scalar.activation(std[:, :], var[:, :], ACT.Sqrt).then_inc(s["std_ready"], 1)

            def modulate(m, i, hTf, hTh=None):
                for b in range(NB):
                    act.wait_ge(s["xn_turned"], 2 * m + b + 1)
                    for t in range(4, KT):
                        last = nc.scalar.activation(hTf[:, t, b * P:b * P + P], ps[:, 4 + 2 * b + t // 4, (t % 4) * P:(t % 4 + 1) * P],
                                                    ACT.Identity, scale=scp[:, i, t, b:b + 1],
                                                    bias=mcol[:, i // 2, 24 * (i % 2) + t, b:b + 1])
                    last.then_inc(s["hT_by_scalar"], 1)
                    if hTh is None:
                        continue
                    act.wait_ge(s["hT_by_scalar"], 2 * m + b + 1)
                    act.wait_ge(s["hT_by_vector"], 2 * m + b + 1)
                    nc.scalar.activation(hTh[:, :, b * P:b * P + P], hTf[:, :, b * P:b * P + P], ACT.Copy)\
                        .then_inc(s["h_hi_ready"], 1)

            mod_split(MOD0, 0)
            norm(0)
            act.wait_ge(s["scp_ready"], 1)
            modulate(0, 0, hTf0, hTh0)

            def copy_proj(i):
                kind, _ = WIN_ORDER[i]
                act.wait_ge(s["weights_used"], used(WIN + 2 * i + 1))
                b0 = 4 * (i % 2)
                if kind == "b":
                    out, scale = b_ch[:, 4 * i:4 * i + 4], 1.0
                else:
                    out, scale = {"aq": (qTA, DH_A ** -0.5), "ak": (kTA, 1.0), "av": (vA, 1.0), "z": (z, 1.0)}[kind]
                    out = out[:, :, :]
                src = ps[:, b0:b0 + 2, :] if kind in ("av", "z") else ps[:, b0:b0 + 4, 0:256]
                nc.scalar.activation(out, src, ACT.Copy, scale=scale).then_inc(s["proj_saved"], 1)

            for i in range(len(WIN_ORDER)):
                for h in range(2):
                    n = WIN + 2 * i + h
                    split_hi(act, n, n, n // RAW + 1)
                if i:
                    copy_proj(i - 1)
            copy_proj(len(WIN_ORDER) - 1)
            mod_split(MOD1, 1)

            act.wait_ge(s["soft_in"], 1)
            act.wait_ge(s["small_loaded"], 64)
            step(nc.scalar.activation(sm[:, 3], sm[:, 1], ACT.Exp, scale=-1.0))
            nc.scalar.activation(sm[:, 5, 0:8], alog[:, :], ACT.Exp)
            nc.scalar.activation(sm[:, 6], ab[:, :, 8:16], ACT.Tanh, scale=0.5)
            nc.scalar.activation(sm[:, 4], sm[:, 3], ACT.Ln, bias=1.0).then_inc(s["softplus_l"], 1)
            def conv_tmp(t):
                return (LT if t < 8 else CTa)[:, 2 * (t % 8):2 * (t % 8) + 2]
            act.wait_ge(s["mod_cols_saved"], 9)
            for t in range(12):
                nc.scalar.activation(conv_tmp(t), b_ch[:, t], ACT.Identity, scale=conv_cols[:, 1, t:t + 1])\
                    .then_inc(s["conv_mid"], 1)
            act.wait_ge(s["k_turned"], 1)
            nc.scalar.activation(kcT[:, :, :], ps[:, 4].rearrange("p (a n) -> p a n", n=P), ACT.Copy).then_inc(s["k_saved"], 1)
            nc.scalar.activation(kc[:, :], ps[:, 5], ACT.Copy).then_inc(s["k_saved"], 1)
            act.wait_ge(s["k_saved"], 2)
            act.dma_start(new_k[0, 0].rearrange("t h d -> t (h d)"), kc[:, :]).then_inc(s["state_stored"], 16)
            act.dma_start(new_v[0, 0].rearrange("t h d -> t (h d)"), vA[:, 0]).then_inc(s["state_stored"], 16)
            for j in range(3):
                act.wait_ge(s["conv_sum"], 12 + 4 * j + 4)
                nc.scalar.activation(b_ch[:, 4 * j:4 * j + 4], (LT[:, 8 * j:8 * j + 8] if j < 2 else CTa[:, 0:8])
                                     .rearrange("p (a c) n -> p a (c n)", c=2), ACT.Silu).then_inc(s["conv_done"], 1)
            nc.scalar.activation(z[:, :, :], z[:, :, :], ACT.Silu).then_inc(s["silu_z"], 1)
            act.wait_ge(s["conv_done"], 3)
            act.wait_ge(s["scores_turned"], 3)
            nc.scalar.activation(R.rearrange("p (a c) n -> p a (c n)", c=2), b_ch[:, 0:8], ACT.Square).then_inc(s["sq_ready"], 1)
            act.wait_ge(s["gc_saved"], 1)
            nc.scalar.activation(sm[:, 12], sm[:, 10], ACT.Exp).then_inc(s["egc_ready"], 1)
            nc.scalar.activation(sm[:, 13], sm[:, 11], ACT.Exp).then_inc(s["kdf_ready"], 1)
            PR = (X[:, 0:8], X[:, 8:16], XT[:, 0:8])
            PT = (M1[:, 0:8], M1[:, 8:16], XT[:, 8:16])
            for i in range(3):
                act.wait_ge(s["p_in"], i + 1)
                nc.scalar.activation(PR[i], PR[i], ACT.Exp).then_inc(s["p_exp"], 1)
            for b in range(NB):
                act.wait_ge(s["diff_ready"], b + 1)
                nc.scalar.activation(decay[:, 8 * b:8 * b + 8], decay[:, 8 * b:8 * b + 8], ACT.Exp, scale=-1.0)\
                    .then_inc(s["decay_ready"], 1)
            for i in range(3):
                act.wait_ge(s["p_turned"], i + 1)
                nc.scalar.activation(PT[i].rearrange("p (a c) n -> p a (c n)", c=4), ps[:, 2 * i:2 * i + 2, :], ACT.Copy)\
                    .then_inc(s["pT_saved"], 1)
            act.wait_ge(s["ss_turned"], 1)
            nc.scalar.activation(LT.rearrange("p (a c) n -> p a (c n)", c=4), ps[:, 4:8, :], ACT.Sqrt, bias=eps[:, 0:1])\
                .then_inc(s["rq_ready"], 1)
            act.wait_ge(s["ktok_turned"], 1)
            nc.scalar.activation(b_ch[:, 8:10], ps[:, 6].rearrange("p (a n) -> p a n", a=2), ACT.Copy).then_inc(s["ktok_saved"], 1)
            act.wait_ge(s["L_turned"], 1)
            nc.scalar.activation(LT.rearrange("p (a c) n -> p a (c n)", c=4), ps[:, 4:8, :], ACT.Copy).then_inc(s["LT_saved"], 1)
            act.wait_ge(s["attn_turned"], 1)
            nc.scalar.activation(attn.rearrange("p (a c) n -> p a (c n)", c=4), ps[:, 0:4, :], ACT.Copy).then_inc(s["attnT_saved"], 1)
            with act.Fori(0, LEVELS - 1) as l:
                for g in range(4):
                    act.wait_ge(s["m1_turned"], 4 * l + g + 1)
                    nc.scalar.activation(M1[:, 4 * g:4 * g + 4].rearrange("p a n -> p (a n)"), ps[:, g], ACT.Copy)\
                        .then_inc(s["m1_saved"], 1)
            for g in range(4):
                act.wait_ge(s["vnew_turned"], g + 1)
                nc.scalar.activation(M1[:, 4 * g:4 * g + 4].rearrange("p a n -> p (a n)"), ps[:, g], ACT.Copy)\
                    .then_inc(s["vnew_saved"], 1)
            act.wait_ge(s["o_b_turned"], 2)
            nc.scalar.activation(y[:, 0, 512:1024], ps[:, 4], ACT.Copy).then_inc(s["ob0_ready"], 1)
            act.wait_ge(s["state_turned"], 1)
            nc.scalar.activation(CTa[:, 8:16].rearrange("p (a c) n -> p a (c n)", c=4), ps[:, 0:2, :], ACT.Copy)\
                .then_inc(s["state_saved"], 1)
            act.wait_ge(s["state_saved"], 1)
            act.dma_start(new_state[0, 0].rearrange("d h k v -> k (d h) v"), CTa[:, 8:16]).then_inc(s["state_stored"], 16)
            act.wait_ge(s["yss_ready"], 1)
            nc.scalar.activation(sm[:, 16, 0:8], sm[:, 15, 0:8], ACT.Sqrt).then_inc(s["ystd_ready"], 1)

            def save_gate(i):
                act.wait_ge(s["gates_turned"], i + 1)
                if i:
                    act.wait_ge(s["x_updated"], i)
                nc.scalar.activation(gate_bc.rearrange("p b (h n) -> p (b h) n", n=512), ps[:, 0:4, :], ACT.Copy)\
                    .then_inc(s["gates_saved"], 1)

            act.wait_ge(s["y_turned"], 2)
            act.wait_ge(s["state_stored"], 48)
            for b in range(NB):
                nc.scalar.activation(hTh1[:, :, b * P:b * P + P], ps[:, 2 * b:2 * b + 2, :].rearrange("p a (c n) -> p (a c) n", n=P),
                                     ACT.Copy).then_inc(s["yT_hi"], 1)
            for n in range(WOUT, FFN):
                split_hi(act, n, n, n // RAW + 1)
            save_gate(0)
            norm(1)
            modulate(1, 1, hTf1, hTh1)
            save_gate(1)

            def swiglu(n0, turn0, hbase, nb):
                def save_hidden(cnt):
                    for b in range(nb):
                        act.wait_ge(s["h_turned"], cnt + b + 1)
                        nc.scalar.activation(hcTh[:, :, b * P:b * P + P],
                                             ps[:, 2 * b if nb == 2 else 4, :].rearrange("p (t n) -> p t n", n=P), ACT.Copy)\
                            .then_inc(s["hc_hi"], 1)

                def gate_silu(n_gate):
                    act.wait_ge(s["weights_used"], used(n_gate))
                    for b in range(nb):
                        nc.scalar.activation(sg[:, b], ps[:, 2 * b, :], ACT.Silu).then_inc(s["silu_ready"], 1)

                for k in range(4):
                    split_hi(act, n0 + k, k, turn0 + 1)
                gate_silu(n0 + 1)
                with act.Fori(1, NC) as cc:
                    m = n0 + 6 * cc - 2
                    for k in range(6):
                        if k == 2:
                            save_hidden(hbase + nb * (cc - 1))
                        split_hi(act, m + k, 4 + k, turn0 + cc + (4 + k) // RAW)
                        if k == 3:
                            gate_silu(m + 1)
                split_hi(act, n0 + UNITS_E - 2, 4, turn0 + NC)
                save_hidden(hbase + nb * (NC - 1))
                split_hi(act, n0 + UNITS_E - 1, 5, turn0 + NC)

            swiglu(FFN, FFN // RAW, 0, NB)
            norm(2)
            fetch(poolw[:, :, :], pool_w[0].rearrange("g (t p) n -> p (g t) n", p=P), "poolw_loaded")
            save_gate(2)
            norm(3)
            fetch(w_rt[:, :, :], w_router[0].rearrange("(t p) e -> p t e", p=P), "poolw_loaded")
            modulate(2, 3, hTf1)
            save_gate(3)
            fetch(finalg, final_g.partition_broadcast(P), "finalg_loaded")
            for b in range(NB):
                act.wait_ge(s["htok_turned"], b + 1)
                nc.scalar.activation(htok_h[:, b], ps[:, 4 + 2 * b:6 + 2 * b, :], ACT.Copy).then_inc(s["htok_hi"], 1)
            act.wait_ge(s["route_dd"], 1)
            nc.scalar.activation(rt[:, 5, :, 1:2], rt[:, 5, :, 0:1], ACT.Exp).then_inc(s["route_exp"], 1)

            def save_gathered(q, cnt):
                act.wait_ge(s["gathered_hi"], cnt)
                nc.scalar.activation(hTh1[:, :, q * P:q * P + P].rearrange("p (a c) n -> p a c n", c=4),
                                     ps[:, 6:8, :].rearrange("p a (c n) -> p a c n", n=P), ACT.Copy).then_inc(s["xg_hi"], 1)

            def save_result(n_last):
                act.wait_ge(s["weights_used"], used(n_last))
                nc.scalar.activation(yh.rearrange("p (a n) -> p a n", n=512), ps[:, 2:4, :], ACT.Copy).then_inc(s["y_hi"], 1)

            def expert(n0, turn0, hbase, q, j):
                def save_hidden(cnt):
                    act.wait_ge(s["h_turned"], cnt + 1)
                    nc.scalar.activation(hcTh[:, :, 0:P], ps[:, 4, :].rearrange("p (t n) -> p t n", n=P), ACT.Copy)\
                        .then_inc(s["hc_hi"], 1)

                def gate_silu(n_gate):
                    act.wait_ge(s["weights_used"], used(n_gate))
                    nc.scalar.activation(sg[:, 0], ps[:, 0, :], ACT.Silu).then_inc(s["silu_ready"], 1)

                def chunk(cc, peeled):
                    m = n0 + 6 * cc - 2
                    for k in range(6):
                        if k == 2:
                            save_hidden(hbase + cc - 1)
                            if peeled == 2:
                                save_gathered(1 - q, j + 2)
                        split_hi(act, m + k, 4 + k, turn0 + cc + (4 + k) // RAW)
                        if k == 3:
                            gate_silu(m + 1)

                for k in range(4):
                    split_hi(act, n0 + k, k, turn0 + 1)
                    if k == 1:
                        save_result(n0 - 1)
                gate_silu(n0 + 1)
                chunk(1, 1)
                chunk(2, 2)
                with act.Fori(3, NC) as cc:
                    chunk(cc, 0)
                split_hi(act, n0 + UNITS_E - 2, 4, turn0 + NC)
                save_hidden(hbase + NC - 1)
                split_hi(act, n0 + UNITS_E - 1, 5, turn0 + NC)

            act.wait_ge(s["npass_ready"], 1)
            passes = nc.scalar.value_load(npass[0:1, 0:1], min_val=1, max_val=2)
            save_gathered(0, 1)
            act.wait_ge(s["result_zeroed"], 1)
            with act.Fori(0, passes) as p:
                with act.Fori(0, N_EXP // 2) as e2:
                    for q in range(2):
                        j = p * N_EXP + e2 * 2 + q
                        expert(MOE + UNITS_E * j, MOE // RAW + NC * j, NB * NC + NC * j, q, j)
            save_result(MOE + UNITS_E * N_EXP * passes - 1)
            norm(4)

        @block.vector
        def _(dve):
            steps = [0]
            VT = nc.vector.tensor_tensor

            def step(ins):
                steps[0] += 1
                ins.then_inc(s["dve_step"], 1)
                dve.wait_ge(s["dve_step"], steps[0])

            dve.wait_ge(s["rows_turned"], 2)
            dve.wait_ge(s["csil_ready"], 1)
            nc.vector.tensor_copy(cols[:, :], ps[:, 7, 0:92])
            step(nc.vector.tensor_copy(flat(bcol), ps[:, 6, 128:224]))
            nc.vector.memset(csp[:, :, :].bitcast(F32), 0.0).then_inc(s["cols_saved"], 1)
            dve.wait_ge(s["csil_ready"], 1)
            dve.wait_ge(s["cols_saved"], 1)
            cs = csil.rearrange("p (b k) -> p k b", b=NB)
            step(nc.vector.tensor_copy(csp[:, :, 0:2], cs))
            VT(csp[:, :, 2:4], cs, csp[:, :, 0:2].bitcast(F32), ALU.subtract).then_inc(s["csplit_ready"], 1)

            def mod_rest(base, l):
                with dve.Fori(0, 4) as i:
                    for k in range(6):
                        split_lo(dve, base + 6 * i + k, base + k)
                    dve.wait_ge(s["mod_cols_turned"], 4 * l + i + 1)
                    VT(mcol[:, l, bass.ds(12 * i, 12), :], ps[:, 3, 0:24].rearrange("p (k b) -> p k b", b=NB),
                       rep(bcol[:, l, bass.ds(12 * i, 12)], 2, NB), ALU.add).then_inc(s["mod_cols_saved"], 1)
                dve.wait_ge(s["mod_cols_saved"], 4 * l + 5)
                for w in range(2):
                    i = 2 * l + w
                    step(nc.vector.scalar_tensor_tensor(scp[:, i], mcol[:, l, 24 * w + 8:24 * w + 16], 1.0,
                                                        rep(ng_cols[:, i], 2, NB), ALU.add, ALU.mult))
                    g = mcol[:, l, 24 * w + 16:24 * w + 24]
                    if l == 1 and w == 0:
                        step(VT(gcol[:, i], g, rep(pscale_cols, 2, NB), ALU.mult))
                    else:
                        step(nc.vector.tensor_copy(gcol[:, i], g))
                dve.sem_inc(s["scp_ready"], 1)
                dve.sem_inc(s["gcol_ready"], 1)

            def norm(i, normalise=True):
                xn = xn0 if i == 0 else xn1
                dve.wait_ge(s["sumsq_ready"], 2 * i + 2)
                nc.vector.tensor_scalar(var[:, :], sumsq[:, :], 1.0 / D, EPS, ALU.mult, ALU.add).then_inc(s["var_ready"], 1)
                dve.wait_ge(s["std_ready"], i + 1)
                step(nc.vector.reciprocal(rstd[:, :], std[:, :]))
                if normalise:
                    for b in range(NB):
                        nc.vector.tensor_scalar(xn[:, b], x[:, b], rstd[:, b:b + 1], None, ALU.mult).then_inc(s["xn_ready"], 1)

            def modulate(m, i, hTf, hTh=None, hTl=None):
                for b in range(NB):
                    dve.wait_ge(s["xn_turned"], 2 * m + b + 1)
                    for t in range(4):
                        last = nc.vector.tensor_scalar(hTf[:, t, b * P:b * P + P], ps[:, 4 + 2 * b, t * P:t * P + P],
                                                       scp[:, i, t, b:b + 1], mcol[:, i // 2, 24 * (i % 2) + t, b:b + 1],
                                                       ALU.mult, ALU.add)
                    last.then_inc(s["hT_by_vector"], 1)
                for b in range(NB if hTh is not None else 0):
                    dve.wait_ge(s["h_hi_ready"], 2 * m + b + 1)
                    VT(hTl[:, :, b * P:b * P + P], hTf[:, :, b * P:b * P + P], hTh[:, :, b * P:b * P + P].bitcast(F32),
                       ALU.subtract).then_inc(s["h_lo_ready"], 1)

            dve.sem_inc(s["mod_cols_saved"], 1)
            mod_rest(MOD0, 0)
            norm(0)
            modulate(0, 0, hTf0, hTh0, hTl0)
            dve.wait_ge(s["ab_turned"], 1)
            nc.vector.tensor_copy(ab.rearrange("p b n -> p (b n)"), ps[:, 7, 0:32]).then_inc(s["ab_saved"], 1)
            for i in range(2 * len(WIN_ORDER)):
                split_lo(dve, WIN + i, WIN + i)
            mod_rest(MOD1, 1)

            def col(i):
                return sm[:, i]
            dve.wait_ge(s["small_loaded"], 64)
            step(VT(col(0).rearrange("p (b n) -> p b n", b=NB), ab[:, :, 0:8], rep(dtb[:, :], 1, NB), ALU.add))
            nc.vector.tensor_scalar(col(2), col(0), 0.0, None, ALU.max)
            nc.vector.scalar_tensor_tensor(col(1), col(0), -1.0, col(0), ALU.mult, ALU.max).then_inc(s["soft_in"], 1)
            dve.wait_ge(s["softplus_l"], 1)
            dve.wait_ge(s["soft_in"], 1)
            nc.vector.tensor_scalar(col(9), col(6), 0.5, 0.5, ALU.mult, ALU.add).then_inc(s["beta_ready"], 1)
            step(VT(col(7), col(2), col(4), ALU.add))
            nc.vector.scalar_tensor_tensor(col(8).rearrange("p (b n) -> p b n", b=NB), col(7).rearrange("p (b n) -> p b n", b=NB),
                                           -1.0, rep(sm[:, 5, 0:8], 1, NB), ALU.mult, ALU.mult).then_inc(s["g_ready"], 1)
            def conv_tmp(t):
                return (LT if t < 8 else CTa)[:, 2 * (t % 8):2 * (t % 8) + 2]
            for tap in (0, 2):
                for t in range(12):
                    if tap == 0:
                        dve.wait_ge(s["conv_mid"], t + 1)
                    elif t == 0:
                        dve.wait_ge(s["conv_sum"], 12)
                    src = b_ch[:, t].rearrange("p (b n) -> p b n", b=NB)
                    dst, src = ((conv_tmp(t)[:, :, 1:P], src[:, :, 0:P - 1]) if tap == 0 else
                                (conv_tmp(t)[:, :, 0:P - 1], src[:, :, 1:P]))
                    nc.vector.scalar_tensor_tensor(dst, src, conv_cols[:, tap, t:t + 1], dst, ALU.mult, ALU.add)\
                        .then_inc(s["conv_sum"], 1)
            dve.wait_ge(s["gc_turned"], 1)
            step(nc.vector.tensor_copy(col(10), ps[:, 6, 0:16]))
            VT(col(11), ps[:, 6, 16:32], col(10), ALU.subtract).then_inc(s["gc_saved"], 1)
            for b in range(NB):
                dve.wait_ge(s["gcrow_turned"], b + 1)
                for d in range(2):
                    cut = slice(8 * b + 4 * d, 8 * b + 4 * d + 4)
                    last = VT(decay[:, cut], ps[:, 6 + d].rearrange("p (h n) -> p h n", n=P),
                              rep(sm[:, 10, cut], 2, P), ALU.subtract)
                step(last)
                nc.vector.tensor_scalar(decay[:, 8 * b:8 * b + 8], decay[:, 8 * b:8 * b + 8], 0.0, None, ALU.max)\
                    .then_inc(s["diff_ready"], 1)
            PR = (X[:, 0:8], X[:, 8:16], XT[:, 0:8])
            mx = sm[:, 18:21].rearrange("p a (c n) -> p (a c) n", n=8)
            den = sm[:, 21:23].rearrange("p a (c n) -> p (a c) n", n=8)
            dve.wait_ge(s["bias_masked"], 1)
            for i in range(3):
                dve.wait_ge(s["scores_turned"], i + 1)
                nc.vector.tensor_reduce(mx[:, i], ps[:, 2 * i:2 * i + 2, :].rearrange("p a (c n) -> p (a c) n", n=P),
                                        AX.X, ALU.max).then_inc(s["mx_ready"], 1)
            dve.wait_ge(s["mx_ready"], 3)
            step(VT(mx[:, 3], mx[:, 1], mx[:, 2], ALU.max))
            for i in range(3):
                VT(PR[i], ps[:, 2 * i:2 * i + 2, :].rearrange("p a (c n) -> p (a c) n", n=P),
                   rep(mx[:, 0 if i == 0 else 3], 2, P), ALU.subtract).then_inc(s["p_in"], 1)
            for i in range(3):
                dve.wait_ge(s["p_exp"], i + 1)
                last = nc.vector.tensor_reduce(den[:, i], PR[i], AX.X, ALU.add)
            step(last)
            step(VT(den[:, 1], den[:, 1], den[:, 2], ALU.add))
            step(nc.vector.reciprocal(den[:, 0:2], den[:, 0:2]))
            for b in range(NB):
                dve.wait_ge(s["o_turned"], b + 1)
                for par in range(2):
                    last = VT(y[:, b, 0:512].rearrange("p (a r n) -> p a r n", r=2, n=DH_A)[:, :, par],
                              ps[:, b].rearrange("p (a r n) -> p a r n", r=2, n=DH_A)[:, :, par],
                              rep(den[:, b, 4 * par:4 * par + 4], 2, DH_A), ALU.mult)
                last.then_inc(s["oa_ready"], 1)
            dve.wait_ge(s["rq_ready"], 1)
            step(nc.vector.reciprocal(LT[:, :, :], LT[:, :, :]))
            qv = b_ch[:, 0:4].rearrange("p a (c n) -> p (a c) n", n=P)
            kv = b_ch[:, 4:8].rearrange("p a (c n) -> p (a c) n", n=P)
            nc.vector.scalar_tensor_tensor(qv, qv, DK ** -0.5, LT[:, 0:8], ALU.mult, ALU.mult).then_inc(s["qn_ready"], 1)
            VT(kv, kv, LT[:, 8:16], ALU.mult).then_inc(s["kn_ready"], 1)
            dve.wait_ge(s["v_turned"], 1)
            dve.wait_ge(s["beta_ready"], 1)
            dve.wait_ge(s["gc_saved"], 1)

            def bank(i):
                return ps[:, i].rearrange("p (h n) -> p h n", n=P)
            for d in range(2):
                VT(R[:, 4 * d:4 * d + 4], bank(4), rep(sm[:, 9, 4 * d:4 * d + 4], 2, P), ALU.mult)
            dve.wait_ge(s["ks_turned"], 1)
            dve.wait_ge(s["egc_ready"], 1)
            for d in range(2):
                last = VT(R[:, 8 + 4 * d:12 + 4 * d], bank(6 + d), rep(sm[:, 12, 8 + 4 * d:12 + 4 * d], 2, P), ALU.mult)
            step(last)
            for d in range(2):
                last = VT(R[:, 8 + 4 * d:12 + 4 * d], bank(5), R[:, 8 + 4 * d:12 + 4 * d], ALU.subtract)
            step(last)
            VT(R[:, 8:16], R[:, 8:16], rep(sm[:, 9, 8:16], 2, P), ALU.mult).then_inc(s["rhs_ready"], 1)
            for b in range(NB):
                dve.wait_ge(s["decay_ready"], b + 1)
                for d in range(2):
                    cut = slice(8 * b + 4 * d, 8 * b + 4 * d + 4)
                    last = VT(attn[:, cut], bank(2 + b), decay[:, cut], ALU.mult)
                step(last)
                for d in range(2):
                    cut = slice(8 * b + 4 * d, 8 * b + 4 * d + 4)
                    last = VT(decay[:, cut], bank(b), decay[:, cut], ALU.mult)
                step(last)
                VT(decay[:, 8 * b:8 * b + 8], decay[:, 8 * b:8 * b + 8], rep(sm[:, 9, 8 * b:8 * b + 8], 2, P), ALU.mult)\
                    .then_inc(s["L_beta"], 1)
            dve.wait_ge(s["x1_tmp"], 8)
            for g in range(4):
                cut = slice(4 * g, 4 * g + 4)
                VT(X[:, cut], rep(ident[:, :], 1, 4), X[:, cut], ALU.subtract)
                VT(XT[:, cut], rep(ident[:, :], 1, 4), XT[:, cut], ALU.subtract).then_inc(s["xx_saved"], 1)
            with dve.Fori(0, LEVELS - 1) as l:
                dve.wait_ge(s["xx_saved"], 4 * l + 4)
                for g in range(4):
                    cut = slice(4 * g, 4 * g + 4)
                    dve.wait_ge(s["xx_turned"], 4 * l + g + 1)
                    VT(X[:, cut], X[:, cut], bank(4 + 2 * (g % 2)), ALU.subtract)
                    VT(XT[:, cut], XT[:, cut], bank(5 + 2 * (g % 2)), ALU.subtract).then_inc(s["xx_saved"], 1)
            dve.wait_ge(s["qs_turned"], 1)
            for d in range(2):
                last = VT(R[:, 4 * d:4 * d + 4], bank(6 + d), rep(sm[:, 12, 8 + 4 * d:12 + 4 * d], 2, P), ALU.mult)
            step(last)
            yb1 = y[:, 1, 512:1024].rearrange("p (h n) -> p h n", n=P)
            step(VT(yb1, bank(5), R[:, 0:4], ALU.add))
            step(VT(yb1, yb1, R[:, 4:8], ALU.add))
            dve.wait_ge(s["ob0_ready"], 1)
            for b in range(NB):
                yb = y[:, b, 512:1024].rearrange("p (h n) -> p h n", n=P)
                last = VT(R[:, 8 + 4 * b:12 + 4 * b], yb, yb, ALU.mult)
            step(last)
            step(nc.vector.tensor_reduce(sm[:, 14, 0:8], R[:, 8:16], AX.X, ALU.add))
            nc.vector.tensor_scalar(sm[:, 15, 0:8], sm[:, 14, 0:8], 1.0 / DK, EPS, ALU.mult, ALU.add).then_inc(s["yss_ready"], 1)
            dve.wait_ge(s["ystd_ready"], 1)
            dve.wait_ge(s["z_gained"], 1)
            step(nc.vector.reciprocal(sm[:, 17, 0:8], sm[:, 16, 0:8]))
            for b in range(NB):
                yb = y[:, b, 512:1024].rearrange("p (h n) -> p h n", n=P)
                last = VT(yb, yb, rep(sm[:, 17, 4 * b:4 * b + 4], 2, P), ALU.mult)
            step(last)
            VT(y[:, :, 512:1024], y[:, :, 512:1024], z[:, :, :], ALU.mult).then_inc(s["yb_ready"], 1)

            for b in range(NB):
                dve.wait_ge(s["yT_hi"], b + 1)
                VT(hTl1[:, :, b * P:b * P + P], ps[:, 2 * b:2 * b + 2, :].rearrange("p a (c n) -> p (a c) n", n=P),
                   hTh1[:, :, b * P:b * P + P].bitcast(F32), ALU.subtract).then_inc(s["yT_lo"], 1)
            for n in range(WOUT, FFN):
                split_lo(dve, n, n)

            def update(i, n_last):
                dve.wait_ge(s["gates_saved"], i + 1)
                if n_last is not None:
                    dve.wait_ge(s["weights_used"], used(n_last))
                for b in range(NB):
                    for h in range(2):
                        last = VT(tmp[:, h], ps[:, 4 + 2 * b + h, :], gate_bc[:, b, 512 * h:512 * h + 512], ALU.mult)
                    step(last)
                    xb = x[:, b].rearrange("p (h n) -> p h n", n=512)
                    step(VT(xb, xb, tmp[:, :, :], ALU.add))
                dve.sem_inc(s["x_updated"], 1)

            update(0, FFN - 1)
            norm(1)
            modulate(1, 1, hTf1, hTh1, hTl1)

            def swiglu(n0, hbase, nb):
                def save_hidden(cnt):
                    for b in range(nb):
                        dve.wait_ge(s["hc_hi"], cnt + b + 1)
                        VT(hcTl[:, :, b * P:b * P + P], ps[:, 2 * b if nb == 2 else 4, :].rearrange("p (t n) -> p t n", n=P),
                           hcTh[:, :, b * P:b * P + P].bitcast(F32), ALU.subtract).then_inc(s["hc_lo"], 1)

                def hidden(n_up, cnt):
                    dve.wait_ge(s["weights_used"], used(n_up))
                    for b in range(nb):
                        dve.wait_ge(s["silu_ready"], cnt + b + 1)
                        VT(hc[:, b], sg[:, b], ps[:, 2 * b + 1, :], ALU.mult).then_inc(s["h_ready"], 1)

                for k in range(4):
                    split_lo(dve, n0 + k, k)
                hidden(n0 + 3, hbase)
                with dve.Fori(1, NC) as cc:
                    m = n0 + 6 * cc - 2
                    for k in range(6):
                        if k == 2:
                            save_hidden(hbase + nb * (cc - 1))
                        split_lo(dve, m + k, 4 + k)
                    hidden(m + 3, hbase + nb * cc)
                split_lo(dve, n0 + UNITS_E - 2, 4)
                save_hidden(hbase + nb * (NC - 1))
                split_lo(dve, n0 + UNITS_E - 1, 5)

            swiglu(FFN, 0, NB)
            update(1, MOE - 1)
            dve.wait_ge(s["counts_turned"], 1)
            step(nc.vector.reciprocal(tmp[:, 0], ps[:, 3]))
            step(VT(flat(band), flat(band), tmp[:, 0], ALU.mult))
            VT(band[:, :, :], band[:, :, :], rep(ident[:, :], 1, 4), ALU.subtract).then_inc(s["band_scaled"], 1)
            norm(2)
            for b in range(NB):
                dve.wait_ge(s["pooled"], b + 1)
                VT(hTf1[:, :, b * P:b * P + P], ps[:, 2 * b:2 * b + 2, :].rearrange("p a (c n) -> p (a c) n", n=P),
                   rep(scp[:, 2, :, b], 2, P), ALU.mult).then_inc(s["yp_ready"], 1)
            dve.wait_ge(s["pool_mixed"], 1)
            update(2, None)
            norm(3)
            modulate(2, 3, hTf1)
            dve.wait_ge(s["logits_turned"], 1)
            step(nc.vector.tensor_copy(rt[:, 0].rearrange("p b e -> p (b e)"), ps[:, 0, 0:16]))
            for b in range(NB):
                last = nc.vector.max(rt[:, 1, b], rt[:, 0, b])
            step(last)
            for b in range(NB):
                last = nc.vector.max_index(idx8[:, b], rt[:, 1, b], rt[:, 0, b])
            step(last)
            VT(rt[:, 5, :, 0:1], rt[:, 1, :, 1:2], rt[:, 1, :, 0:1], ALU.subtract).then_inc(s["route_dd"], 1)
            step(nc.vector.tensor_copy(rt[:, 2], idx8[:, :, :]))
            for i in range(2):
                last = VT(rt[:, 3 + i], rep(iota[:, 0:N_EXP], 1, NB), rt[:, 2, :, i:i + 1].broadcast_to([P, NB, N_EXP]), ALU.is_equal)
            step(last)
            step(VT(rt[:, 7], rt[:, 3], rt[:, 4], ALU.add))
            dve.sem_inc(s["mask_ready"], 1)
            dve.wait_ge(s["route_exp"], 1)
            step(nc.vector.tensor_scalar(rt[:, 5, :, 2:3], rt[:, 5, :, 1:2], 1.0, None, ALU.add))
            step(nc.vector.reciprocal(rt[:, 5, :, 3:4], rt[:, 5, :, 2:3]))
            step(VT(rt[:, 5, :, 4:5], rt[:, 5, :, 3:4], rt[:, 5, :, 1:2], ALU.mult))
            for i in range(2):
                last = VT(rt[:, 8 + i], rt[:, 3 + i], rt[:, 5, :, 3 + i:4 + i].broadcast_to([P, NB, N_EXP]), ALU.mult)
            step(last)
            step(VT(rt[:, 10], rt[:, 8], rt[:, 9], ALU.add))
            dve.wait_ge(s["pos_turned"], 1)
            step(nc.vector.scalar_tensor_tensor(rt[:, 11].rearrange("p b e -> p (b e)"), ps[:, 1, 0:16], 1.0,
                                                rt[:, 7].rearrange("p b e -> p (b e)"), ALU.add, ALU.mult))
            for q in range(NB):
                cut = slice(N_EXP * q, N_EXP * q + N_EXP)
                nc.vector.tensor_scalar(posj[:, cut].rearrange("p e b -> p b e"), rt[:, 11], -1.0 - P * q, None, ALU.add)
                nc.vector.tensor_copy(gatej[:, cut].rearrange("p e b -> p b e"), rt[:, 10])
            step(nc.vector.tensor_reduce(rt[:, 12, 0, 0:1], ps[:, 1, 16:24], AX.X, ALU.max))
            nc.vector.tensor_scalar(npass[:, :], rt[:, 12, 0, 0:1], float(P), 1.0, ALU.is_gt, ALU.add).then_inc(s["npass_ready"], 1)
            for b in range(NB):
                dve.wait_ge(s["htok_hi"], b + 1)
                VT(htok_l[:, b], ps[:, 4 + 2 * b:6 + 2 * b, :].rearrange("p a n -> p (a n)"), htok_h[:, b].bitcast(F32),
                   ALU.subtract).then_inc(s["htok_lo"], 1)

            def slots(j):
                VT(ST[:, :, :], rep(iota[:, :], 1, NB), posj[:, j, :].unsqueeze(2).broadcast_to([P, NB, P]),
                   ALU.is_equal).then_inc(s["st_ready"], 1)

            def save_gathered(q, cnt):
                dve.wait_ge(s["gathered_lo"], cnt)
                nc.vector.tensor_copy(hTl1[:, :, q * P:q * P + P].rearrange("p (a c) n -> p a c n", c=4),
                                      ps[:, 6:8, :].rearrange("p a (c n) -> p a c n", n=P)).then_inc(s["xg_lo"], 1)

            def save_result(cnt):
                dve.wait_ge(s["y_hi"], cnt)
                VT(yl.rearrange("p (a n) -> p a n", n=512), ps[:, 2:4, :],
                   yh.rearrange("p (a n) -> p a n", n=512).bitcast(F32), ALU.subtract).then_inc(s["y_lo"], 1)

            def collect(b, cnt):
                dve.wait_ge(s["scattered"], cnt)
                out = acc[:, b].rearrange("p (h n) -> p h n", n=512)
                nc.vector.scalar_tensor_tensor(out, ps[:, 6:8, :], gcur[:, b:b + 1], out, ALU.mult, ALU.add)\
                    .then_inc(s["acc_added"], 1)

            def expert(n0, hbase, q, j):
                def save_hidden(cnt):
                    dve.wait_ge(s["hc_hi"], cnt + 1)
                    VT(hcTl[:, :, 0:P], ps[:, 4, :].rearrange("p (t n) -> p t n", n=P),
                       hcTh[:, :, 0:P].bitcast(F32), ALU.subtract).then_inc(s["hc_lo"], 1)

                def hidden(n_up, cnt):
                    dve.wait_ge(s["weights_used"], used(n_up))
                    dve.wait_ge(s["silu_ready"], cnt + 1)
                    VT(hc[:, 0], sg[:, 0], ps[:, 1, :], ALU.mult).then_inc(s["h_ready"], 1)

                def chunk(cc, peeled):
                    m = n0 + 6 * cc - 2
                    for k in range(6):
                        if k == 2:
                            save_hidden(hbase + cc - 1)
                            if peeled == 1:
                                collect(0, 2 * j + 1)
                        if k == 4 and peeled == 1:
                            collect(1, 2 * j + 2)
                            dve.wait_ge(s["acc_added"], 2 * j + 2)
                            nc.vector.tensor_copy(Sm.rearrange("p b n -> p (b n)"), ps[:, 5, 0:NB * P])
                            nc.vector.tensor_copy(gcur[:, :], gatej[:, j, :]).then_inc(s["s_saved"], 1)
                        if k == 4 and peeled == 2:
                            save_gathered(1 - q, j + 2)
                        if not (peeled == 1 and k == 0):
                            split_lo(dve, m + k, 4 + k)
                    hidden(m + 3, hbase + cc)

                for k in range(4):
                    split_lo(dve, n0 + k, k)
                    if k == 1:
                        save_result(j + 1)
                        slots(j + 1)
                split_lo(dve, n0 + 4, 4)
                hidden(n0 + 3, hbase)
                chunk(1, 1)
                chunk(2, 2)
                with dve.Fori(3, NC) as cc:
                    chunk(cc, 0)
                split_lo(dve, n0 + UNITS_E - 2, 4)
                save_hidden(hbase + NC - 1)
                split_lo(dve, n0 + UNITS_E - 1, 5)

            dve.wait_ge(s["npass_ready"], 1)
            passes = nc.vector.value_load(npass[0:1, 0:1], min_val=1, max_val=2)
            dve.wait_ge(s["acc_zeroed"], 1)
            slots(0)
            save_gathered(0, 1)
            with dve.Fori(0, passes) as p:
                with dve.Fori(0, N_EXP // 2) as e2:
                    for q in range(2):
                        j = p * N_EXP + e2 * 2 + q
                        expert(MOE + UNITS_E * j, NB * NC + NC * j, q, j)
            save_result(passes * N_EXP + 1)
            collect(0, passes * (2 * N_EXP) + 1)
            collect(1, passes * (2 * N_EXP) + 2)
            dve.wait_ge(s["acc_added"], passes * (2 * N_EXP) + 2)
            dve.wait_ge(s["gates_saved"], 4)
            for b in range(NB):
                step(VT(acc[:, b], acc[:, b], gate_bc[:, b], ALU.mult))
                step(VT(x[:, b], x[:, b], acc[:, b], ALU.add))
            dve.sem_inc(s["x_updated"], 1)
            norm(4, normalise=False)
            dve.wait_ge(s["finalg_loaded"], 16)
            for b in range(NB):
                last = nc.vector.scalar_tensor_tensor(xn1[:, b], x[:, b], rstd[:, b:b + 1], finalg, ALU.mult, ALU.mult)
            last.then_inc(s["y_ready"], 1)

        @block.tensor
        def _(pe):
            MM = nc.tensor.matmul

            def turn(out, src, n=P):
                return nc.tensor.transpose(out, src, ident[0:n, 0:n])

            pe.sem_inc(s["weights_used"], SPLIT)
            pe.wait_ge(s["consts_ready"], 1)
            pe.wait_ge(s["rows_loaded"], 96)
            turn(ps[:, 7, 0:92], rowsA[0:92, :], 92).then_inc(s["rows_turned"], 1)
            turn(ps[:, 6, 128:224], rowsB[0:96, :], 96).then_inc(s["rows_turned"], 1)

            def mod(base, l):
                with pe.Fori(0, 4) as i:
                    for j in range(3):
                        for h in range(2):
                            n = base + 6 * i + 2 * j + h
                            k = (base + 2 * j + h) % SPLIT
                            pe.wait_ge(s["lo_ready"], n + 1)
                            for t in range(4):
                                MM(ps[:, j, :], csp[:, 4 * h + t, :], w_hi[:, k, t, :], start=h == 0 and t == 0, stop=False)
                                last = MM(ps[:, j, :], csp[:, 4 * h + t, :], w_lo[:, k, t, :], start=False,
                                          stop=h == 1 and t == 3)
                            last.then_inc(s["weights_used"], 1)
                    pe.wait_ge(s["mod_rows_copied"], 12 * l + 3 * i + 3)
                    pe.wait_ge(s["mod_cols_saved"], 4 * l + i + 1)
                    for j in range(3):
                        for t in range(4):
                            o = 2 * (4 * j + t)
                            last = MM(ps[:, 3, o:o + 2], m4[0:4, j, t * P:t * P + P], fold[0:4, :], start=True, stop=True)
                    last.then_inc(s["mod_cols_turned"], 1)

            def turn_xn(m, nidx, xn):
                for b in range(NB):
                    pe.wait_ge(s["xn_ready"], 2 * nidx + b + 1)
                    for t in range(KT):
                        last = turn(ps[:, 4 + 2 * b + t // 4, (t % 4) * P:(t % 4 + 1) * P], xn[:, b, t * P:t * P + P])
                    last.then_inc(s["xn_turned"], 1)

            pe.wait_ge(s["csplit_ready"], 1)
            mod(MOD0, 0)
            turn_xn(0, 0, xn0)

            pe.wait_ge(s["h_lo_ready"], 2)
            pe.wait_ge(s["small_loaded"], 64)
            for b in range(NB):
                for t in range(KT):
                    last = MM(ps[:, 7, 16 * b:16 * b + 16], hTf0[:, t, b * P:b * P + P], w_ab[:, t, :], start=t == 0, stop=t == KT - 1)
            last.then_inc(s["ab_turned"], 1)
            for i, (kind, _) in enumerate(WIN_ORDER):
                b0 = 4 * (i % 2)
                if i == 1:
                    pe.wait_ge(s["ab_saved"], 1)
                if i >= 2:
                    pe.wait_ge(s["proj_saved"], i - 1)
                for h in range(2):
                    n = WIN + 2 * i + h
                    if kind in ("av", "z"):
                        multiply(pe, n, n, hTh0, hTl0, 4 * h, [(0, b0), (1, b0 + 1)], h == 0, h == 1)
                        continue
                    pe.wait_ge(s["lo_ready"], n + 1)
                    for q in range(4):
                        out = ps[:, b0 + q, 0:256]
                        for t in range(4):
                            kt = 4 * h + t
                            wh = w_hi[:, n % SPLIT, t, q * P:q * P + P]
                            MM(out, wh, hTh0[:, kt, :], start=kt == 0, stop=False)
                            MM(out, wh, hTl0[:, kt, :], start=False, stop=False)
                            last = MM(out, w_lo[:, n % SPLIT, t, q * P:q * P + P], hTh0[:, kt, :], start=False, stop=kt == KT - 1)
                    last.then_inc(s["weights_used"], 1)
            pe.wait_ge(s["proj_saved"], 7)
            mod(MOD1, 1)

            pe.wait_ge(s["cache_loaded"], 48)
            for i in range(4):
                turn(ps[:, 4, i * P:i * P + P], kc[:, i * P:i * P + P])
            for i in range(4):
                last = turn(ps[:, 5, i * P:i * P + P], kTA[:, i, 0:P])
            last.then_inc(s["k_turned"], 1)
            pe.wait_ge(s["g_ready"], 1)
            pe.wait_ge(s["tri_ready"], 1)
            g3 = sm[:, 8].rearrange("p (b d h) -> p b d h", b=NB, d=2)
            o3 = ps[:, 6, 0:16].rearrange("p (b d h) -> p b d h", b=NB, d=2)
            for d in range(2):
                MM(o3[:, :, d], tri[:, 1 - d], g3[:, :, d], start=True, stop=True)
            MM(ps[:, 6, 16:32], ones[:, :], sm[:, 8], start=True, stop=True).then_inc(s["gc_turned"], 1)
            def scores(q_blk, kT, k0, bank0, biased):
                if biased:
                    for par in range(2):
                        MM(ps[:, bank0 + par, :], rev[:, :], bias.rearrange("p (a r) n -> p r a n", r=2)[:, par], start=True, stop=False)
                for a in range(4):
                    for par in range(2):
                        rowsl = slice(64 * par, 64 * par + 64)
                        last = MM(ps[:, bank0 + par, a * P:a * P + P], qTA[rowsl, a, q_blk * P:q_blk * P + P],
                                  kT[rowsl, a, k0:k0 + P], start=not biased, stop=not biased or a == 3)
                last.then_inc(s["scores_turned"], 1)
            scores(0, kTA, 0, 0, False)
            pe.wait_ge(s["bias_masked"], 1)
            scores(1, kTA, P, 2, True)
            pe.wait_ge(s["k_saved"], 2)
            scores(1, kcT, 0, 4, False)
            pe.wait_ge(s["grep_ready"], 1)
            pe.wait_ge(s["gc_saved"], 1)
            for b in range(NB):
                if b:
                    pe.wait_ge(s["diff_ready"], b)
                for i in range(8):
                    last = MM(ps[:, 6 + i // 4, (i % 4) * P:(i % 4 + 1) * P], attn[:, 8 * b + i], tri[:, 1 - i // 4], start=True, stop=True)
                last.then_inc(s["gcrow_turned"], 1)
            PR = (X[:, 0:8], X[:, 8:16], XT[:, 0:8])
            PT = (M1[:, 0:8], M1[:, 8:16], XT[:, 8:16])
            pe.wait_ge(s["p_exp"], 3)
            for i in range(3):
                for h in range(8):
                    last = turn(ps[:, 2 * i + h // 4, (h % 4) * P:(h % 4 + 1) * P], PR[i][:, h])
                last.then_inc(s["p_turned"], 1)
            pe.wait_ge(s["pT_saved"], 3)
            for b in range(NB):
                for h in range(H_A):
                    at = 4 * (h % 2) + h // 2
                    cut = slice(h * DH_A, h * DH_A + DH_A)
                    last = MM(ps[:, b, cut], PT[b][:, at], vA[:, b, cut], start=True, stop=b == 0)
                    if b:
                        last = MM(ps[:, b, cut], PT[2][:, at], vc[:, cut], start=False, stop=True)
                last.then_inc(s["o_turned"], 1)
            pe.wait_ge(s["sq_ready"], 1)
            pe.wait_ge(s["diff_ready"], 2)
            for i in range(4):
                last = MM(ps[:, 4 + i, :], ones[:, :], R[:, 4 * i:4 * i + 4].rearrange("p a n -> p (a n)"), start=True, stop=True)
            last.then_inc(s["ss_turned"], 1)
            def tile(i, h, b):
                return b_ch[:, 4 * i + h, b * P:b * P + P]
            pe.wait_ge(s["kn_ready"], 1)
            pe.wait_ge(s["oa_ready"], 2)
            for b in range(NB):
                for h in range(H_B):
                    MM(ps[:, b, h * P:h * P + P], tile(1, h, b), tile(1, h, b), start=True, stop=True)
                    MM(ps[:, 2 + b, h * P:h * P + P], tile(0, h, b), tile(1, h, b), start=True, stop=True)
            for b in range(NB):
                for h in range(H_B):
                    last = turn(ps[:, 4 + b, h * P:h * P + P], tile(2, h, b))
            last.then_inc(s["v_turned"], 1)
            for h in range(H_B):
                last = turn(ps[:, 6, h * P:h * P + P], tile(1, h, 0))
            last.then_inc(s["ktok_turned"], 1)
            pe.wait_ge(s["ktok_saved"], 1)
            for d in range(2):
                for h in range(H_B):
                    last = MM(ps[:, 6 + d, h * P:h * P + P], tile(1, h, 1), s0[:, d, h], start=True, stop=True)
            last.then_inc(s["ks_turned"], 1)
            pe.wait_ge(s["rhs_ready"], 1)
            pe.wait_ge(s["L_masked"], 2)
            for i in range(16):
                last = turn(ps[:, 4 + i // 4, (i % 4) * P:(i % 4 + 1) * P], decay[:, i])
            last.then_inc(s["L_turned"], 1)
            pe.wait_ge(s["attn_masked"], 2)
            for i in range(16):
                last = turn(ps[:, i // 4, (i % 4) * P:(i % 4 + 1) * P], attn[:, i])
            last.then_inc(s["attn_turned"], 1)
            pe.wait_ge(s["attnT_saved"], 1)
            with pe.Fori(0, (LEVELS - 1) // 2) as r:
                for half in range(2):
                    l = 2 * r + half
                    ct = (CTa, decay)[half]

                    def m1(g):
                        pe.wait_ge(s["xx_saved"], 4 * l + g + 1)
                        if g % 2 == 0:
                            pe.wait_ge(s["ct_ready"], 2 * l + g // 2 + 1)
                        for i in range(4 * g, 4 * g + 4):
                            last = MM(ps[:, g, (i % 4) * P:(i % 4 + 1) * P], ct[:, i], X[:, i], start=True, stop=True)
                        last.then_inc(s["m1_turned"], 1)

                    def xx(g):
                        pe.wait_ge(s["m1_saved"], 4 * l + g + 1)
                        pe.wait_ge(s["xx_saved"], 4 * l + g + 3)
                        for i in range(4 * g, 4 * g + 4):
                            cut = slice((i % 4) * P, (i % 4 + 1) * P)
                            MM(ps[:, 4 + 2 * (g % 2), cut], XT[:, i], M1[:, i], start=True, stop=True)
                            last = MM(ps[:, 5 + 2 * (g % 2), cut], M1[:, i], XT[:, i], start=True, stop=True)
                        last.then_inc(s["xx_turned"], 1)
                    m1(0)
                    m1(1)
                    xx(0)
                    m1(2)
                    xx(1)
                    m1(3)
                    xx(2)
                    xx(3)
            for g in range(4):
                pe.wait_ge(s["xx_saved"], 4 * LEVELS - 4 + g + 1)
                for i in range(4 * g, 4 * g + 4):
                    last = MM(ps[:, g, (i % 4) * P:(i % 4 + 1) * P], XT[:, i], R[:, i], start=True, stop=True)
                last.then_inc(s["vnew_turned"], 1)
            for b in range(NB):
                pe.wait_ge(s["vnew_saved"], 2 * b + 2)
                for h in range(H_B):
                    for d in range(2):
                        i = 8 * b + 4 * d + h
                        last = MM(ps[:, 4 + b, h * P:h * P + P], attn[:, i], M1[:, i], start=d == 0, stop=d == 1)
                last.then_inc(s["o_b_turned"], 1)
            for d in range(2):
                for h in range(H_B):
                    last = MM(ps[:, 6 + d, h * P:h * P + P], tile(0, h, 1), s0[:, d, h], start=True, stop=True)
            last.then_inc(s["qs_turned"], 1)
            pe.wait_ge(s["kd_ready"], 2)
            for i in range(8):
                last = MM(ps[:, i // 4, (i % 4) * P:(i % 4 + 1) * P], CTa[:, i], M1[:, i], start=True, stop=True)
            last.then_inc(s["state_turned"], 1)

            pe.wait_ge(s["yb_ready"], 1)
            pe.wait_ge(s["state_saved"], 1)
            for b in range(NB):
                for t in range(KT):
                    last = turn(ps[:, 2 * b + t // 4, (t % 4) * P:(t % 4 + 1) * P], y[:, b, t * P:t * P + P])
                last.then_inc(s["y_turned"], 1)
            pe.wait_ge(s["yT_lo"], 2)
            for n in range(WOUT, FFN):
                h, cc = (n - WOUT) % 2, (n - WOUT) // 2
                multiply(pe, n, n, hTh1, hTl1, 4 * h, [(0, 4 + cc), (1, 6 + cc)], h == 0, h == 1)

            def gates(i):
                for q in range(4):
                    pe.wait_ge(s["diag_ready"], 4 * i + q + 1)
                    last = MM(ps[:, q, :], ones[:, :], diag[:, q].rearrange("p a n -> p (a n)"), start=True, stop=True)
                last.then_inc(s["gates_turned"], 1)

            gates(0)
            turn_xn(1, 1, xn1)
            pe.wait_ge(s["h_lo_ready"], 4)
            gates(1)
            pe.wait_ge(s["gates_saved"], 2)
            pe.wait_ge(s["zr_ready"], 1)

            def swiglu(n0, hbase, nb, xh, xl, before_last=None):
                down = [(b, (4 + 2 * b) if nb == 2 else 2) for b in range(nb)]

                def gate_up(m, start_k):
                    for k in range(4):
                        banks = [(b, 2 * b + k // 2) for b in range(nb)]
                        multiply(pe, m + k, start_k + k, xh, xl, 4 * (k % 2), banks, k % 2 == 0, k % 2 == 1)

                def down_proj(m, start_k, stop=False):
                    for k in range(2):
                        multiply(pe, m + k, start_k + k, hcTh, hcTl, 0, [(b, bk + k) for b, bk in down], False, stop)

                def turn_hidden(cnt):
                    for b in range(nb):
                        pe.wait_ge(s["h_ready"], cnt + b + 1)
                        for t in range(4):
                            last = turn(ps[:, 2 * b if nb == 2 else 4, t * P:t * P + P], hc[:, b, t * P:t * P + P])
                        last.then_inc(s["h_turned"], 1)

                for _, bk in down:
                    for k in range(2):
                        MM(ps[:, bk + k, :], zr[:, 0:P], zr[:, P:P + 512], start=True, stop=False)
                gate_up(n0, 0)
                turn_hidden(hbase)
                with pe.Fori(1, NC) as cc:
                    m = n0 + 6 * cc - 2
                    if nb == 2:
                        pe.wait_ge(s["hc_lo"], hbase + nb * cc)
                    gate_up(m, 4)
                    pe.wait_ge(s["hc_lo"], hbase + nb * cc)
                    down_proj(m + 4, 8)
                    turn_hidden(hbase + nb * cc)
                if before_last is not None:
                    before_last()
                pe.wait_ge(s["hc_lo"], hbase + nb * NC)
                down_proj(n0 + UNITS_E - 2, 4, stop=True)

            swiglu(FFN, 0, NB, hTh1, hTl1)

            pe.wait_ge(s["band_ready"], 1)
            MM(ps[:, 3, :], ones[:, :], flat(band), start=True, stop=True).then_inc(s["counts_turned"], 1)
            pe.wait_ge(s["band_scaled"], 1)
            for b in range(NB):
                pe.wait_ge(s["xn_ready"], 4 + b + 1)
                for t in range(KT):
                    last = MM(ps[:, 2 * b + t // 4, (t % 4) * P:(t % 4 + 1) * P], xn1[:, b, t * P:t * P + P], band[:, t // 2],
                              start=True, stop=True)
                last.then_inc(s["pooled"], 1)
            pe.wait_ge(s["poolw_loaded"], 16)
            for b in range(NB):
                pe.wait_ge(s["yp_ready"], b + 1)
                for g in range(4):
                    for t in range(2):
                        last = MM(ps[:, 4 + 2 * b + g // 2, (g % 2) * 256:(g % 2 + 1) * 256], hTf1[:, 2 * g + t, b * P:b * P + P],
                                  poolw[:, 2 * g + t, :], start=t == 0, stop=t == 1)
            last.then_inc(s["pool_mixed"], 1)
            gates(2)
            turn_xn(2, 3, xn1)
            gates(3)
            pe.wait_ge(s["hT_by_vector"], 6)
            pe.wait_ge(s["hT_by_scalar"], 6)
            pe.wait_ge(s["gates_saved"], 4)
            pe.wait_ge(s["poolw_loaded"], 32)
            for b in range(NB):
                for t in range(KT):
                    last = MM(ps[:, 0, 8 * b:8 * b + 8], hTf1[:, t, b * P:b * P + P], w_rt[:, t, :], start=t == 0, stop=t == KT - 1)
            last.then_inc(s["logits_turned"], 1)
            for b in range(NB):
                for t in range(KT):
                    last = turn(ps[:, 4 + 2 * b + t // 4, (t % 4) * P:(t % 4 + 1) * P], hTf1[:, t, b * P:b * P + P])
                last.then_inc(s["htok_turned"], 1)
            pe.wait_ge(s["mask_ready"], 1)
            MM(ps[:, 1, 0:8], sup[:, :], rt[:, 7, 0], start=True, stop=True)
            MM(ps[:, 1, 8:16], ones[:, :], rt[:, 7, 0], start=True, stop=False)
            MM(ps[:, 1, 8:16], sup[:, :], rt[:, 7, 1], start=False, stop=True)
            MM(ps[:, 1, 16:24], ones[:, :], rt[:, 7, 0], start=True, stop=False)
            MM(ps[:, 1, 16:24], ones[:, :], rt[:, 7, 1], start=False, stop=True).then_inc(s["pos_turned"], 1)

            def gather_hi(cnt):
                pe.wait_ge(s["st_ready"], cnt)
                for b in range(NB):
                    turn(ps[:, 5, b * P:b * P + P], ST[:, b].bitcast(F32))
                gather_part(htok_h, "gathered_hi")

            def gather_part(tok, name):
                for t in range(KT):
                    for b in range(NB):
                        last = MM(ps[:, 6 + t // 4, (t % 4) * P:(t % 4 + 1) * P], tok[:, b, t * P:t * P + P], ST[:, b],
                                  start=b == 0, stop=b == 1)
                last.then_inc(s[name], 1)

            def scatter(b):
                for h in range(2):
                    MM(ps[:, 6 + h, :], Sm[:, b], yh[:, 512 * h:512 * h + 512], start=True, stop=False)
                    last = MM(ps[:, 6 + h, :], Sm[:, b], yl[:, 512 * h:512 * h + 512], start=False, stop=True)
                last.then_inc(s["scattered"], 1)

            def expert(n0, hbase, q, j):
                def gate_up(m, start_k, k_from, k_to):
                    for k in range(k_from, k_to):
                        multiply(pe, m + k, start_k + k, hTh1, hTl1, 4 * (k % 2), [(q, k // 2)], k % 2 == 0, k % 2 == 1)

                def down_proj(m, start_k, stop=False):
                    for k in range(2):
                        multiply(pe, m + k, start_k + k, hcTh, hcTl, 0, [(0, 2 + k)], False, stop)

                def turn_hidden(cnt):
                    pe.wait_ge(s["h_ready"], cnt + 1)
                    for t in range(4):
                        last = turn(ps[:, 4, t * P:t * P + P], hc[:, 0, t * P:t * P + P])
                    last.then_inc(s["h_turned"], 1)

                pe.wait_ge(s["xg_hi"], j + 1)
                pe.wait_ge(s["xg_lo"], j + 1)
                gate_up(n0, 0, 0, 4)
                pe.wait_ge(s["y_lo"], j + 1)
                scatter(0)
                for k in range(2):
                    MM(ps[:, 2 + k, :], zr[:, 0:P], zr[:, P:P + 512], start=True, stop=False)
                turn_hidden(hbase)
                for cc in (1, 2):
                    m = n0 + 6 * cc - 2
                    gate_up(m, 4, 0, 2)
                    if cc == 1:
                        pe.wait_ge(s["acc_added"], 2 * j + 1)
                        scatter(1)
                    else:
                        pe.wait_ge(s["xg_hi"], j + 2)
                        gather_part(htok_l, "gathered_lo")
                    gate_up(m, 4, 2, 4)
                    pe.wait_ge(s["hc_lo"], hbase + cc)
                    down_proj(m + 4, 8)
                    turn_hidden(hbase + cc)
                    if cc == 1:
                        pe.wait_ge(s["s_saved"], j + 1)
                        gather_hi(j + 2)
                with pe.Fori(3, NC) as cc:
                    m = n0 + 6 * cc - 2
                    gate_up(m, 4, 0, 4)
                    pe.wait_ge(s["hc_lo"], hbase + cc)
                    down_proj(m + 4, 8)
                    turn_hidden(hbase + cc)
                pe.wait_ge(s["hc_lo"], hbase + NC)
                down_proj(n0 + UNITS_E - 2, 4, stop=True)

            pe.wait_ge(s["npass_ready"], 1)
            passes = nc.tensor.value_load(npass[0:1, 0:1], min_val=1, max_val=2)
            pe.wait_ge(s["htok_lo"], 2)
            gather_hi(1)
            pe.wait_ge(s["xg_hi"], 1)
            gather_part(htok_l, "gathered_lo")
            for k in range(2):
                last = MM(ps[:, 2 + k, :], zr[:, 0:P], zr[:, P:P + 512], start=True, stop=True)
            last.then_inc(s["result_zeroed"], 1)
            with pe.Fori(0, passes) as p:
                with pe.Fori(0, N_EXP // 2) as e2:
                    for q in range(2):
                        j = p * N_EXP + e2 * 2 + q
                        expert(MOE + UNITS_E * j, NB * NC + NC * j, q, j)
            pe.wait_ge(s["y_lo"], passes * N_EXP + 1)
            scatter(0)
            pe.wait_ge(s["acc_added"], passes * (2 * N_EXP) + 1)
            scatter(1)


_INS = ["x_prompt", "x_sample", "cache_k_ctx", "cache_v_ctx", "state_delta", "c", "c_ctx", "w_mod", "b_mod", "norm_g",
        "final_g", "w_in", "conv_w", "a_log", "dt_bias", "rpb", "o_gain", "w_out", "ffn_gate", "ffn_up", "ffn_down",
        "pool_w", "pool_scale", "w_router", "moe_gate", "moe_up", "moe_down"]
_OUTS = [(1, 128, 1024), (1, 128, 1024), (1, 1, 128, 8, 64), (1, 1, 128, 8, 64), (1, 1, 2, 4, 128, 128)]


def kernel(**inputs):
    import numpy as _np
    import concourse.bacc as _bacc
    from concourse import mybir as _mybir
    from concourse.bass_utils import run_bass_kernel_spmd as _run

    nc = _bacc.Bacc("TRN2", target_bir_lowering=False, num_devices=1, dynamic_dma_scratch_size=64)
    arrays, args = {}, []
    for name in _INS:
        a = _np.ascontiguousarray(inputs[name])
        arrays[f"in_{name}"] = a
        args.append(nc.dram_tensor(f"in_{name}", a.shape, _mybir.dt.from_np(a.dtype), kind="ExternalInput").ap())
    for i, shape in enumerate(_OUTS):
        args.append(nc.dram_tensor(f"out_{i}", shape, _mybir.dt.float32, kind="ExternalOutput").ap())
    build(nc, *args)
    r = _run(nc, [arrays], core_ids=[0])
    return tuple(r.results[0][f"out_{i}"] for i in range(len(_OUTS)))
```

```python
from contextlib import ExitStack

import concourse.bass as bass
from concourse import mybir

F32 = mybir.dt.float32
R32 = mybir.dt.float32r
I32 = mybir.dt.int32
U32 = mybir.dt.uint32
BF16 = mybir.dt.bfloat16
ALU = mybir.AluOpType
ACT = mybir.ActivationFunctionType
AX = mybir.AxisListType

P = 128
D = 1024
KT = D // P
NB = 2
H_A, DH_A, A_W = 8, 64, 512
H_B, DK, B_W = 4, 128, 512
GRID_W = 64
NA_KW = 16
NROW = P // GRID_W
CONV_K = 3
D_FF = 3584
NC = D_FF // 512
N_EXP = 8
POOL_WINDOWS = (2, 4, 8, 16)
POOL_G = 256
EPS = 1e-6
NEG = -1e30
RAW = 6
SPLIT = 3
LEVELS = 7

MOD_FIRST = 4
MOD_WIN = 6
MOD_FFN = MOD_FIRST + MOD_WIN
WIN = 2 * MOD_FIRST
WOUT = WIN + 14 + 2 * MOD_WIN
FFN = WOUT + 4
FFN_CHUNK = 6 + 4
MOE = FFN + 4 + 4 + FFN_CHUNK * (NC - 1) + 2
UNROLL = 3
UNITS_E = 6 * NC
assert MOD_FFN + 2 * NC == 24 and (NC - 1) % UNROLL == 0
assert FFN_CHUNK * UNROLL % RAW == 0 and MOE % RAW == 0 and UNITS_E % RAW == 0

WIN_ORDER = (("b", 3), ("b", 4), ("b", 5), ("aq", 0), ("ak", 1), ("av", 2), ("z", 6))

SEMS = """LT_saved L_beta L_masked L_turned ab_saved ab_turned acc_added acc_zeroed act_step attnT_saved
attn_masked attn_turned band_ready band_scaled beta_ready bias_loaded bias_masked cache_loaded
cols_saved consts_ready conv_done conv_mid conv_sum counts_turned csil_ready csplit_ready ct_ready
decay_ready diag_ready diff_ready dve_step egc_ready finalg_loaded g_ready gates_saved gates_turned
gathered_hi gathered_lo gc_saved gc_turned gcrow_turned grep_ready hT_by_scalar
hT_by_vector h_hi_ready h_lo_ready h_ready h_turned hc_hi hc_lo hi_ready htok_hi htok_lo
htok_turned k_saved k_turned kd_ready kdf_ready kn_ready ks_turned ktok_saved ktok_turned lo_ready
len_diag len_inverse len_turned logits_turned m1_saved m1_turned mask_ready mod_cols_saved mod_cols_turned mod_rows_copied mx_ready
npass_ready o_b_turned o_turned oa_ready ob0_ready pT_saved p_exp p_in p_turned pgate_ready pool_mixed
pool_step pooled poolw_loaded pos_turned proj_saved qk_turned qn_ready qs_turned result_zeroed rhs_ready
route_dd route_exp rows_loaded rows_turned rq_ready s_saved scattered scores_turned scp_ready
silu_ready silu_z small_loaded soft_in softplus_l sq_ready ss_turned st_ready state_saved
state_stored state_turned std_ready sumsq_ready tri_ready v_turned var_ready vnew_saved vnew_turned
weights_used x1_tmp x_loaded x_updated xg_hi xg_lo xn_ready xn_turned xx_saved xx_turned yT_hi
yT_lo y_hi y_lo y_ready y_stored y_turned yb_ready yp_ready yss_ready ystd_ready z_gained zr_ready""".split()


def win_unit(i, h=0):
    return WIN + 4 * i + h


def mod_unit(f, h=0):
    return 2 * f + h if f < MOD_FIRST else WIN + 4 * (f - MOD_FIRST) + 2 + h


def ffn_unit(u):
    return FFN + 8 + FFN_CHUNK * u


def rep(ap, axis, n):
    shape = list(ap.shape)
    shape.insert(axis, n)
    return ap.unsqueeze(axis).broadcast_to(shape)


def build(nc, x_prompt, x_sample, cache_k, cache_v, state0, c, c_ctx, w_mod, b_mod, norm_g, final_g,
          w_in, conv_w, a_log, dt_bias, rpb, o_gain, w_out, ffn_gate, ffn_up, ffn_down, pool_w,
          pool_scale, w_router, moe_gate, moe_up, moe_down,
          y_prompt, y_sample, new_k, new_v, new_state):
    top = ExitStack()
    with top:
        def sbuf(stack, name, shape, dt=F32):
            return stack.enter_context(nc.sbuf_tensor(name, [P, *shape], dt))

        s = {n: top.enter_context(nc.semaphore(n)) for n in SEMS}
        raw_full = [top.enter_context(nc.semaphore(f"raw_full{i}")) for i in range(RAW)]
        ps = top.enter_context(nc.psum_tensor("ps", [P, 8, 512], F32))

        raw = sbuf(top, "raw", [RAW, 4, 512])
        w_hi = sbuf(top, "w_hi", [SPLIT, 4, 512], R32)
        w_lo = sbuf(top, "w_lo", [SPLIT, 4, 512], R32)
        x = sbuf(top, "x", [NB, D])
        ident = sbuf(top, "ident", [P])
        ones = sbuf(top, "ones", [P])
        eps = sbuf(top, "eps", [1])
        fold = sbuf(top, "fold", [2])
        rowsA = sbuf(top, "rowsA", [P])
        rowsB = sbuf(top, "rowsB", [P])
        cols = sbuf(top, "cols", [92])
        bcol = sbuf(top, "bcol", [2, 48])
        mcol = sbuf(top, "mcol", [2, 48, NB])
        scp = sbuf(top, "scp", [4, KT, NB])
        pgate = sbuf(top, "pgate", [KT, NB])
        csil = sbuf(top, "csil", [16])
        sumsq = sbuf(top, "sumsq", [NB])
        var = sbuf(top, "var", [NB])
        std = sbuf(top, "std", [NB])
        rstd = sbuf(top, "rstd", [NB])
        c_cols = cols[:, 0:16]
        ng_cols = cols[:, 16:48].rearrange("p (w k) -> p w k", k=KT)
        conv_cols = cols[:, 48:84].rearrange("p (i t) -> p i t", i=CONV_K)
        pscale_cols = cols[:, 84:92]

        mixer = ExitStack()
        tri = sbuf(mixer, "tri", [4, P])
        lev = sbuf(mixer, "lev", [LEVELS, 2, P], BF16)
        b_ch = sbuf(mixer, "b_ch", [12, 256])
        R = sbuf(mixer, "R", [16, P])
        qTA = R[:, 0:8].rearrange("p (a c) n -> p a (c n)", c=2)
        kTA = R[:, 8:16].rearrange("p (a c) n -> p a (c n)", c=2)
        vA = sbuf(mixer, "vA", [NB, 512])
        z = sbuf(mixer, "z", [NB, 512])
        y = sbuf(mixer, "y", [NB, D])
        bias = sbuf(mixer, "bias", [H_A, P])
        rev = sbuf(mixer, "rev", [P])
        kc = sbuf(mixer, "kc", [512])
        vc = sbuf(mixer, "vc", [512])
        kcT = sbuf(mixer, "kcT", [4, P])
        s0 = sbuf(mixer, "s0", [2, H_B, DK])
        ab = sbuf(mixer, "ab", [NB, 16])
        w_ab = sbuf(mixer, "w_ab", [KT, 16])
        sm = sbuf(mixer, "sm", [24, 16])
        ogain = sbuf(mixer, "ogain", [DK])
        alog = sbuf(mixer, "alog", [8])
        dtb = sbuf(mixer, "dtb", [8])
        front = ExitStack()
        csp = sbuf(front, "csp", [KT, P], R32)
        m4 = sbuf(front, "m4", [3, 512])
        xn0 = sbuf(front, "xn0", [NB, D])
        hTf0 = sbuf(front, "hTf0", [KT, 256])
        hTh0 = sbuf(front, "hTh0", [KT, 256], R32)
        hTl0 = sbuf(front, "hTl0", [KT, 256], R32)
        front.close()
        work = ExitStack()
        T = [sbuf(work, f"T{i}", [16, P]) for i in range(7)]
        work.close()
        decay, attn, LT, CTa, X, XT, M1 = T
        mixer.close()

        tail = ExitStack()
        gate_bc = sbuf(tail, "gate_bc", [NB, D])
        diag = sbuf(tail, "diag", [4, 4, P])
        tmp = sbuf(tail, "tmp", [NB, 512])
        xn1 = sbuf(tail, "xn1", [NB, D])
        hTf1 = sbuf(tail, "hTf1", [KT, 256])
        hTh1 = sbuf(tail, "hTh1", [KT, 256], R32)
        hTl1 = sbuf(tail, "hTl1", [KT, 256], R32)
        sg = sbuf(tail, "sg", [NB, 512])
        hc = sbuf(tail, "hc", [NB, 512])
        hcTh = sbuf(tail, "hcTh", [4, 256], R32)
        hcTl = sbuf(tail, "hcTl", [4, 256], R32)
        zr = sbuf(tail, "zr", [640], R32)
        band = sbuf(tail, "band", [4, P])
        pooling = ExitStack()
        poolw = sbuf(pooling, "poolw", [KT, POOL_G])
        m41 = sbuf(pooling, "m41", [2, 512])
        pooling.close()
        htok_h = sbuf(tail, "htok_h", [NB, D], R32)
        htok_l = sbuf(tail, "htok_l", [NB, D], R32)
        yh = sbuf(tail, "yh", [D], R32)
        yl = sbuf(tail, "yl", [D], R32)
        ST = sbuf(tail, "ST", [NB, P], R32)
        Sm = sbuf(tail, "Sm", [NB, P], R32)
        iota = sbuf(tail, "iota", [P])
        sup = sbuf(tail, "sup", [P])
        w_rt = sbuf(tail, "w_rt", [KT, N_EXP])
        rt = sbuf(tail, "rt", [16, NB, N_EXP])
        idx8 = sbuf(tail, "idx8", [NB, 8], U32)
        posj = sbuf(tail, "posj", [NB * N_EXP + 1, NB])
        gatej = sbuf(tail, "gatej", [NB * N_EXP + 1, NB])
        gcur = sbuf(tail, "gcur", [NB])
        npass = sbuf(tail, "npass", [1], I32)
        tail.close()
        acc = xn1
        csp1 = yh.rearrange("p (k n) -> p k n", n=P)
        finalg = diag[:, 0:2].rearrange("p a k n -> p (a k n)")
        block = top.enter_context(nc.Block())

        def flat(t):
            return t.rearrange("p a b -> p (a b)")

        def load(sp, n, k, src, first=False):
            if not first:
                sp.wait_ge(s["lo_ready"], n - RAW + 1)
            sp.dma_start(raw[:, k % RAW], src).then_inc(raw_full[k % RAW], 16)

        def split_hi(act, n, k, turn):
            act.wait_ge(raw_full[k % RAW], 16 * turn)
            act.wait_ge(s["weights_used"], n + 1)
            nc.scalar.activation(w_hi[:, k % SPLIT], raw[:, k % RAW], ACT.Copy).then_inc(s["hi_ready"], 1)

        def split_lo(dve, n, k):
            dve.wait_ge(s["hi_ready"], n + 1)
            nc.vector.tensor_tensor(w_lo[:, k % SPLIT], raw[:, k % RAW], w_hi[:, k % SPLIT].bitcast(F32),
                                    ALU.subtract).then_inc(s["lo_ready"], 1)

        def used(n):
            return n + 1 + SPLIT

        def rows(w, kt0, c0):
            return w.rearrange("(t p) n -> p t n", p=P)[:, kt0:kt0 + 4, bass.ds(c0, 512)]

        def multiply(pe, n, k, xh, xl, kt0, banks, start, stop):
            pe.wait_ge(s["lo_ready"], n + 1)
            for i, (b, bank) in enumerate(banks):
                cut = slice(b * P, b * P + P)
                for t in range(4):
                    st = start and t == 0
                    en = stop and t == 3
                    nc.tensor.matmul(ps[:, bank, :], xh[:, kt0 + t, cut], w_hi[:, k % SPLIT, t, :], start=st, stop=False)
                    nc.tensor.matmul(ps[:, bank, :], xl[:, kt0 + t, cut], w_hi[:, k % SPLIT, t, :], start=False, stop=False)
                    last = nc.tensor.matmul(ps[:, bank, :], xh[:, kt0 + t, cut], w_lo[:, k % SPLIT, t, :],
                                            start=False, stop=en)
            last.then_inc(s["weights_used"], 1)

        @block.sync
        def _(sp):
            for part, src in ((rowsA[0:8, :], c_ctx.rearrange("(k p) -> k p", p=P)),
                              (rowsA[8:16, :], c[0].rearrange("(k p) -> k p", p=P)),
                              (rowsA[16:48, :], norm_g.rearrange("l w (k p) -> (l w k) p", p=P)),
                              (rowsA[48:84, :], conv_w[0].rearrange("i (t p) -> (i t) p", p=P)),
                              (rowsA[84:92, :], pool_scale[0].rearrange("(k p) -> k p", p=P)),
                              (rowsB[0:96, :], b_mod.rearrange("l (k p) -> (l k) p", p=P))):
                sp.dma_start(part, src).then_inc(s["rows_loaded"], 16)
            def mod_load(f):
                for h in range(2):
                    n = mod_unit(f, h)
                    load(sp, n, n, rows(w_mod[0], 4 * h, f * 512), first=n < RAW)

            for f in range(MOD_FIRST):
                mod_load(f)
            for i, (_, ch) in enumerate(WIN_ORDER):
                for h in range(2):
                    n = win_unit(i, h)
                    load(sp, n, n, rows(w_in[0], 4 * h, ch * 512))
                if i < MOD_WIN:
                    mod_load(MOD_FIRST + i)
            for n in range(WOUT, FFN):
                load(sp, n, n, rows(w_out[0], 4 * ((n - WOUT) % 2), (n - WOUT) // 2 * 512))

            def swiglu(n0, gate, up, down):
                for k in range(4):
                    load(sp, n0 + k, k, rows(gate if k < 2 else up, 4 * (k % 2), 0))
                with sp.Fori(1, NC) as cc:
                    m = n0 + 6 * cc - 2
                    for k in range(6):
                        src = (rows(gate if k < 2 else up, 4 * (k % 2), cc * 512) if k < 4 else
                               down.rearrange("(c t p) n -> c p t n", p=P, t=4)[
                                   cc - 1, :, :, (k - 4) * 512:(k - 3) * 512])
                        load(sp, m + k, 4 + k, src)
                for k in range(2):
                    load(sp, n0 + UNITS_E - 2 + k, 4 + k,
                         down.rearrange("(c t p) n -> c p t n", p=P, t=4)[NC - 1, :, :, k * 512:(k + 1) * 512])

            def ffn_gate_up(n, k, c):
                for i in range(4):
                    load(sp, n + i, k + i, rows((ffn_gate if i < 2 else ffn_up)[0], 4 * (i % 2), c * 512))

            def ffn_down_load(n, k, c):
                for i in range(2):
                    load(sp, n + i, k + i,
                         ffn_down[0].rearrange("(c t p) n -> c p t n", p=P, t=4)[c, :, :, i * 512:(i + 1) * 512])

            def mod_pair(n, k, l, c):
                for i in range(4):
                    load(sp, n + i, k + i, rows(w_mod[l], 4 * (i % 2), (c + i // 2) * 512))

            ffn_gate_up(FFN, FFN, 0)
            mod_pair(FFN + 4, FFN + 4, 0, MOD_FFN)
            with sp.Fori(0, (NC - 1) // UNROLL) as r:
                for u in range(UNROLL):
                    k = ffn_unit(u)
                    n = k + FFN_CHUNK * UNROLL * r
                    chunk = UNROLL * r + u + 1
                    ffn_gate_up(n, k, chunk)
                    ffn_down_load(n + 4, k + 4, chunk - 1)
                    mod_pair(n + 6, k + 6, 1, 2 * UNROLL * r + 2 * u)
            ffn_down_load(MOE - 2, MOE - 2, NC - 1)
            with sp.Fori(0, N_EXP) as e:
                swiglu(MOE + UNITS_E * e, moe_gate[0, e], moe_up[0, e], moe_down[0, e])
            sp.wait_ge(s["npass_ready"], 1)
            passes = nc.sync.value_load(npass[0:1, 0:1], min_val=1, max_val=2)
            with sp.If(passes > 1):
                with sp.Fori(0, N_EXP) as e:
                    swiglu(MOE + UNITS_E * N_EXP + UNITS_E * e, moe_gate[0, e], moe_up[0, e], moe_down[0, e])
            sp.wait_ge(s["y_ready"], 1)
            sp.dma_start(y_prompt[0], xn1[:, 0]).then_inc(s["y_stored"], 16)
            sp.dma_start(y_sample[0], xn1[:, 1]).then_inc(s["y_stored"], 16)
            sp.wait_ge(s["y_stored"], 32)
            sp.wait_ge(s["state_stored"], 48)

        @block.gpsimd
        def _(pool):
            steps = [0]

            def step(ins):
                steps[0] += 1
                ins.then_inc(s["pool_step"], 1)
                pool.wait_ge(s["pool_step"], steps[0])

            def keep(ap, pattern, base, mult, fill=0.0, op=ALU.is_ge):
                step(nc.gpsimd.affine_select(out=ap, in_=ap, compare_op=op, fill=fill, base=base,
                                             pattern=pattern, channel_multiplier=mult))

            step(nc.gpsimd.memset(ident[:, :], 0.0))
            keep(ident[:, :], [[-1, P]], 0, 1, fill=1.0, op=ALU.not_equal)
            step(nc.gpsimd.memset(ones[:, :], 1.0))
            step(nc.gpsimd.memset(eps[:, :], EPS))
            nc.gpsimd.tensor_tensor(fold[:, :], ident[:, 0:2], ident[:, 2:4], ALU.add).then_inc(s["consts_ready"], 1)
            step(nc.gpsimd.memset(tri[:, :, :], 1.0))
            keep(tri[:, 0], [[-1, P]], 0, 1)
            keep(tri[:, 1], [[1, P]], 0, -1)
            keep(tri[:, 2], [[-1, P]], -1, 1)
            keep(tri[:, 3], [[1, P]], -1, -1)
            pool.sem_inc(s["tri_ready"], 1)
            step(nc.gpsimd.memset(rev[:, :], 0.0))
            for r in range(NROW):
                cut = slice(r * GRID_W, (r + 1) * GRID_W)
                keep(rev[cut, cut], [[1, GRID_W]], 1 - GRID_W, 1, fill=1.0, op=ALU.not_equal)
            step(nc.gpsimd.memset(lev[:, :, :, :], 0.0))
            for l in range(LEVELS):
                h = 1 << l
                v = lev[:, l].rearrange("p d (b r) -> p d b r", r=2 * h)
                n = P // (2 * h)
                step(nc.gpsimd.memset(v[:, 0, :, h:], 1.0))
                keep(v[:, 0, :, h:], [[-2 * h, n], [0, h]], 0, 1)
                keep(v[:, 0, :, h:], [[2 * h, n], [0, h]], h - 1, -1)
                step(nc.gpsimd.memset(v[:, 1, :, 0:h], 1.0))
                keep(v[:, 1, :, 0:h], [[-2 * h, n], [0, h]], -h, 1)
                keep(v[:, 1, :, 0:h], [[2 * h, n], [0, h]], 2 * h - 1, -1)
            pool.wait_ge(s["bias_loaded"], 64)
            for r in range(NROW):
                v = bias[r * GRID_W:(r + 1) * GRID_W].rearrange("p h (r c) -> p (h r) c", r=NROW)
                hi = GRID_W - NA_KW
                keep(v[:, :, 0:hi], [[0, H_A * NROW], [1, hi]], NA_KW // 2 - GRID_W + 1, 1, fill=NEG)
                keep(v[:, :, NA_KW:], [[0, H_A * NROW], [-1, hi]], GRID_W - 1 + NA_KW // 2 - 1 - NA_KW, -1, fill=NEG)
            pool.sem_inc(s["bias_masked"], 1)

            pool.wait_ge(s["g_ready"], 1)
            pool.wait_ge(s["mod_cols_saved"], MOD_FFN)
            nc.gpsimd.tensor_copy(attn[:, :, :], rep(sm[:, 8], 2, P)).then_inc(s["grep_ready"], 1)
            pool.wait_ge(s["silu_z"], 1)
            nc.gpsimd.tensor_tensor(z.rearrange("p b (h v) -> p (b h) v", v=DK), z.rearrange("p b (h v) -> p (b h) v", v=DK),
                                    rep(ogain[:, :], 1, 8), ALU.mult).then_inc(s["z_gained"], 1)
            pool.wait_ge(s["len_inverse"], 1)
            nc.gpsimd.tensor_tensor(LT[:, 0:8], rep(ident[:, :], 1, 8), rep(sm[:, 17, 0:8], 2, P), ALU.mult)\
                .then_inc(s["len_diag"], 1)
            for b in range(NB):
                pool.wait_ge(s["L_beta"], b + 1)
                v = attn[:, 8 * b:8 * b + 8].rearrange("p (d h) n -> p d h n", d=2)
                nc.gpsimd.tensor_tensor(v, v, rep(tri[:, 0:2], 2, H_B), ALU.mult).then_inc(s["attn_masked"], 1)
            for l in range(1, LEVELS):
                ct = (CTa, decay)[(l - 1) % 2]
                if l == 1:
                    pool.wait_ge(s["LT_saved"], 1)
                if l == 2:
                    pool.wait_ge(s["L_turned"], 1)
                    pool.wait_ge(s["x1_tmp"], 1)
                if l >= 3:
                    pool.wait_ge(s["m1_turned"], 4 * (l - 2))
                for b in range(NB):
                    nc.gpsimd.tensor_tensor(ct[:, 8 * b:8 * b + 8].rearrange("p (d h) n -> p d h n", d=2),
                                            LT[:, 8 * b:8 * b + 8].rearrange("p (d h) n -> p d h n", d=2),
                                            rep(lev[:, l], 2, H_B), ALU.mult).then_inc(s["ct_ready"], 1)
            pool.wait_ge(s["m1_turned"], 20)
            pool.wait_ge(s["kdf_ready"], 1)
            pool.wait_ge(s["ktok_saved"], 1)
            for d in range(2):
                nc.gpsimd.tensor_tensor(CTa[:, 4 * d:4 * d + 4], b_ch[:, 8:10].rearrange("p a (c n) -> p (a c) n", n=P),
                                        rep(sm[:, 13, 4 * d:4 * d + 4], 2, P), ALU.mult).then_inc(s["kd_ready"], 1)

            pool.wait_ge(s["y_turned"], 2)
            pool.wait_ge(s["state_stored"], 48)
            nc.gpsimd.memset(zr[:, :].bitcast(F32), 0.0).then_inc(s["zr_ready"], 1)

            def gates(i):
                pool.wait_ge(s["mod_cols_saved"], (MOD_FFN, MOD_FFN + 1, MOD_FFN + NC, MOD_FFN + NC)[i])
                if i == 2:
                    pool.wait_ge(s["pgate_ready"], 1)
                gate = pgate if i == 2 else mcol[:, i // 2, 24 * (i % 2) + 16:24 * (i % 2) + 24]
                if i:
                    pool.wait_ge(s["gates_turned"], i)
                for b in range(NB):
                    for h in range(2):
                        nc.gpsimd.tensor_tensor(diag[:, 2 * b + h], rep(ident[:, :], 1, 4),
                                                rep(gate[:, 4 * h:4 * h + 4, b], 2, P), ALU.mult)\
                            .then_inc(s["diag_ready"], 1)

            gates(0)
            gates(1)
            step(nc.gpsimd.memset(band[:, :, :], 1.0))
            for i, w in enumerate(POOL_WINDOWS):
                keep(band[:, i], [[-1, P]], w // 2, 1)
                keep(band[:, i], [[1, P]], w - w // 2 - 1, -1)
            step(nc.gpsimd.memset(sup[:, :], 1.0))
            keep(sup[:, :], [[1, P]], -1, -1)
            step(nc.gpsimd.memset(posj[:, :, :], -1.0))
            step(nc.gpsimd.memset(gatej[:, :, :], 0.0))
            nc.gpsimd.iota(iota[:, :], pattern=[[1, P]], base=0, channel_multiplier=0,
                           allow_small_or_imprecise_dtypes=True).then_inc(s["band_ready"], 1)
            gates(2)
            gates(3)
            pool.wait_ge(s["xn_turned"], 6)
            nc.gpsimd.memset(Sm[:, :, :].bitcast(F32), 0.0)
            nc.gpsimd.memset(gcur[:, :], 0.0)
            nc.gpsimd.memset(acc[:, :, :], 0.0).then_inc(s["acc_zeroed"], 1)

        @block.scalar
        def _(act):
            steps = [0]

            def step(ins):
                steps[0] += 1
                ins.then_inc(s["act_step"], 1)
                act.wait_ge(s["act_step"], steps[0])

            def fetch(dst, src, name):
                act.dma_start(dst, src).then_inc(s[name], 16)

            act.wait_ge(s["rows_loaded"], 96)
            fetch(x[:, 0], x_prompt[0], "x_loaded")
            fetch(x[:, 1], x_sample[0], "x_loaded")
            fetch(w_ab[:, :, :], w_in[0].rearrange("(t p) n -> p t n", p=P)[:, :, 7 * 512:7 * 512 + 16], "small_loaded")
            fetch(alog[:, :], a_log[0].rearrange("d h -> (d h)").partition_broadcast(P), "small_loaded")
            fetch(dtb[:, :], dt_bias[0].rearrange("d h -> (d h)").partition_broadcast(P), "small_loaded")
            fetch(ogain[:, :], o_gain[0].partition_broadcast(P), "small_loaded")
            fetch(s0[:, :, :, :], state0[0, 0].rearrange("d h k v -> k d h v"), "cache_loaded")
            fetch(kc[:, :], cache_k[0, 0].rearrange("t h d -> t (h d)"), "cache_loaded")
            fetch(vc[:, :], cache_v[0, 0].rearrange("t h d -> t (h d)"), "cache_loaded")
            nh, nr, nd = rpb.shape[1:]
            for qr in range(NROW):
                for kr in range(NROW):
                    src = bass.AP(tensor=rpb.tensor, offset=(nr // 2 + kr - qr) * nd + nd // 2 - (GRID_W - 1),
                                  ap=[[1, GRID_W], [nr * nd, nh], [1, GRID_W]])
                    fetch(bias[qr * GRID_W:(qr + 1) * GRID_W, :, kr * GRID_W:(kr + 1) * GRID_W], src, "bias_loaded")

            act.wait_ge(s["rows_turned"], 1)
            nc.scalar.activation(csil[:, :], ps[:, 7, 0:16], ACT.Silu).then_inc(s["csil_ready"], 1)

            def copy_row(n, m, j, bank):
                act.wait_ge(s["weights_used"], used(n))
                nc.scalar.activation(m[0:4, j], ps[0:4, bank, :], ACT.Copy).then_inc(s["mod_rows_copied"], 1)

            def norm(i):
                xn = xn0 if i == 0 else xn1
                if i == 0:
                    act.wait_ge(s["x_loaded"], 32)
                else:
                    act.wait_ge(s["x_updated"], i)
                for b in range(NB):
                    nc.scalar.activation(xn[:, b], x[:, b], ACT.Square, accum_out=sumsq[:, b:b + 1])\
                        .then_inc(s["sumsq_ready"], 1)
                act.wait_ge(s["var_ready"], i + 1)
                nc.scalar.activation(std[:, :], var[:, :], ACT.Sqrt).then_inc(s["std_ready"], 1)

            def modulate(m, i, hTf, hTh=None):
                for b in range(NB):
                    act.wait_ge(s["xn_turned"], 2 * m + b + 1)
                    for t in range(4, KT):
                        last = nc.scalar.activation(hTf[:, t, b * P:b * P + P], ps[:, 4 + 2 * b + t // 4, (t % 4) * P:(t % 4 + 1) * P],
                                                    ACT.Identity, scale=scp[:, i, t, b:b + 1],
                                                    bias=mcol[:, i // 2, 24 * (i % 2) + t, b:b + 1])
                    last.then_inc(s["hT_by_scalar"], 1)
                    if hTh is None:
                        continue
                    act.wait_ge(s["hT_by_scalar"], 2 * m + b + 1)
                    act.wait_ge(s["hT_by_vector"], 2 * m + b + 1)
                    nc.scalar.activation(hTh[:, :, b * P:b * P + P], hTf[:, :, b * P:b * P + P], ACT.Copy)\
                        .then_inc(s["h_hi_ready"], 1)

            for f in range(MOD_FIRST + 1):
                for h in range(2 if f < MOD_FIRST else 0):
                    n = mod_unit(f, h)
                    split_hi(act, n, n, n // RAW + 1)
                if f:
                    copy_row(mod_unit(f - 1, 1), m4, (f - 1) % 3, (f - 1) % 3)
            norm(0)
            act.wait_ge(s["scp_ready"], 1)
            modulate(0, 0, hTf0, hTh0)

            def copy_proj(i):
                kind, _ = WIN_ORDER[i]
                act.wait_ge(s["weights_used"], used(win_unit(i, 1)))
                b0 = 4 * (i % 2)
                if kind == "b":
                    out, scale = b_ch[:, 4 * i:4 * i + 4], 1.0
                else:
                    out, scale = {"aq": (qTA, DH_A ** -0.5), "ak": (kTA, 1.0), "av": (vA, 1.0), "z": (z, 1.0)}[kind]
                    out = out[:, :, :]
                src = ps[:, b0:b0 + 2, :]
                if kind not in ("av", "z"):
                    src = src.rearrange("p a (c n) -> p (a c) n", n=256)
                nc.scalar.activation(out, src, ACT.Copy, scale=scale).then_inc(s["proj_saved"], 1)

            for i in range(len(WIN_ORDER)):
                f = MOD_FIRST + i
                split_hi(act, win_unit(i), win_unit(i), win_unit(i) // RAW + 1)
                if i:
                    copy_proj(i - 1)
                split_hi(act, win_unit(i, 1), win_unit(i, 1), win_unit(i, 1) // RAW + 1)
                if i < MOD_WIN:
                    split_hi(act, mod_unit(f), mod_unit(f), mod_unit(f) // RAW + 1)
                if i:
                    copy_row(mod_unit(f - 1, 1), m4, (f - 1) % 3, 2)
                if i < MOD_WIN:
                    split_hi(act, mod_unit(f, 1), mod_unit(f, 1), mod_unit(f, 1) // RAW + 1)
            copy_proj(len(WIN_ORDER) - 1)

            act.wait_ge(s["soft_in"], 1)
            act.wait_ge(s["small_loaded"], 64)
            step(nc.scalar.activation(sm[:, 3], sm[:, 1], ACT.Exp, scale=-1.0))
            nc.scalar.activation(sm[:, 5, 0:8], alog[:, :], ACT.Exp)
            nc.scalar.activation(sm[:, 6], ab[:, :, 8:16], ACT.Tanh, scale=0.5)
            nc.scalar.activation(sm[:, 4], sm[:, 3], ACT.Ln, bias=1.0).then_inc(s["softplus_l"], 1)
            def conv_tmp(t):
                return (LT if t < 8 else CTa)[:, 2 * (t % 8):2 * (t % 8) + 2]
            act.wait_ge(s["mod_cols_saved"], MOD_FFN)
            for t in range(12):
                nc.scalar.activation(conv_tmp(t), b_ch[:, t], ACT.Identity, scale=conv_cols[:, 1, t:t + 1])\
                    .then_inc(s["conv_mid"], 1)
            act.wait_ge(s["k_turned"], 1)
            nc.scalar.activation(kcT[:, :, :], ps[:, 4].rearrange("p (a n) -> p a n", n=P), ACT.Copy).then_inc(s["k_saved"], 1)
            nc.scalar.activation(kc[:, :], ps[:, 5], ACT.Copy).then_inc(s["k_saved"], 1)
            act.wait_ge(s["k_saved"], 2)
            act.dma_start(new_k[0, 0].rearrange("t h d -> t (h d)"), kc[:, :]).then_inc(s["state_stored"], 16)
            act.dma_start(new_v[0, 0].rearrange("t h d -> t (h d)"), vA[:, 0]).then_inc(s["state_stored"], 16)
            for j in range(3):
                act.wait_ge(s["conv_sum"], 12 + 4 * j + 4)
                nc.scalar.activation(b_ch[:, 4 * j:4 * j + 4], (LT[:, 8 * j:8 * j + 8] if j < 2 else CTa[:, 0:8])
                                     .rearrange("p (a c) n -> p a (c n)", c=2), ACT.Silu).then_inc(s["conv_done"], 1)
            nc.scalar.activation(z[:, :, :], z[:, :, :], ACT.Silu).then_inc(s["silu_z"], 1)
            act.wait_ge(s["conv_done"], 3)
            act.wait_ge(s["scores_turned"], 3)
            nc.scalar.activation(R.rearrange("p (a c) n -> p a (c n)", c=2), b_ch[:, 0:8], ACT.Square).then_inc(s["sq_ready"], 1)
            act.wait_ge(s["gc_saved"], 1)
            nc.scalar.activation(sm[:, 12], sm[:, 10], ACT.Exp).then_inc(s["egc_ready"], 1)
            nc.scalar.activation(sm[:, 13], sm[:, 11], ACT.Exp).then_inc(s["kdf_ready"], 1)
            PR = (X[:, 0:8], X[:, 8:16], XT[:, 0:8])
            PT = (M1[:, 0:8], M1[:, 8:16], XT[:, 8:16])
            act.wait_ge(s["ss_turned"], 1)
            nc.scalar.activation(sm[:, 16], ps[:, 6, 0:16], ACT.Sqrt, bias=eps[:, 0:1]).then_inc(s["rq_ready"], 1)
            for i in range(3):
                act.wait_ge(s["p_in"], i + 1)
                nc.scalar.activation(PR[i], PR[i], ACT.Exp).then_inc(s["p_exp"], 1)
            for b in range(NB):
                act.wait_ge(s["diff_ready"], b + 1)
                nc.scalar.activation(decay[:, 8 * b:8 * b + 8], decay[:, 8 * b:8 * b + 8], ACT.Exp, scale=-1.0)\
                    .then_inc(s["decay_ready"], 1)
            for i in range(3):
                act.wait_ge(s["p_turned"], i + 1)
                nc.scalar.activation(PT[i].rearrange("p (a c) n -> p a (c n)", c=4), ps[:, 2 * i:2 * i + 2, :], ACT.Copy)\
                    .then_inc(s["pT_saved"], 1)
            for n in range(WOUT, WOUT + SPLIT):
                split_hi(act, n, n, n // RAW + 1)
            act.wait_ge(s["ktok_turned"], 1)
            nc.scalar.activation(b_ch[:, 8:10], ps[:, 6].rearrange("p (a n) -> p a n", a=2), ACT.Copy).then_inc(s["ktok_saved"], 1)
            act.wait_ge(s["L_turned"], 1)
            nc.scalar.activation(LT.rearrange("p (a c) n -> p a (c n)", c=4), ps[:, 0:4, :], ACT.Copy).then_inc(s["LT_saved"], 1)
            act.wait_ge(s["attn_turned"], 1)
            nc.scalar.activation(attn.rearrange("p (a c) n -> p a (c n)", c=4), ps[:, 4:8, :], ACT.Copy).then_inc(s["attnT_saved"], 1)
            with act.Fori(0, LEVELS - 1) as l:
                for g in range(4):
                    act.wait_ge(s["m1_turned"], 4 * l + g + 1)
                    nc.scalar.activation(M1[:, 4 * g:4 * g + 4].rearrange("p a n -> p (a n)"), ps[:, g], ACT.Copy)\
                        .then_inc(s["m1_saved"], 1)
            for g in range(4):
                act.wait_ge(s["vnew_turned"], g + 1)
                nc.scalar.activation(M1[:, 4 * g:4 * g + 4].rearrange("p a n -> p (a n)"), ps[:, g], ACT.Copy)\
                    .then_inc(s["vnew_saved"], 1)
            act.wait_ge(s["o_b_turned"], 2)
            nc.scalar.activation(y[:, 0, 512:1024], ps[:, 4], ACT.Copy).then_inc(s["ob0_ready"], 1)
            act.wait_ge(s["state_turned"], 1)
            nc.scalar.activation(CTa[:, 8:16].rearrange("p (a c) n -> p a (c n)", c=4), ps[:, 0:2, :], ACT.Copy)\
                .then_inc(s["state_saved"], 1)
            act.wait_ge(s["state_saved"], 1)
            act.dma_start(new_state[0, 0].rearrange("d h k v -> k (d h) v"), CTa[:, 8:16]).then_inc(s["state_stored"], 16)
            act.wait_ge(s["yss_ready"], 1)
            nc.scalar.activation(sm[:, 16, 0:8], sm[:, 15, 0:8], ACT.Sqrt).then_inc(s["ystd_ready"], 1)

            def save_gate(i):
                act.wait_ge(s["gates_turned"], i + 1)
                if i:
                    act.wait_ge(s["x_updated"], i)
                nc.scalar.activation(gate_bc.rearrange("p b (h n) -> p (b h) n", n=512), ps[:, 0:4, :], ACT.Copy)\
                    .then_inc(s["gates_saved"], 1)

            act.wait_ge(s["y_turned"], 2)
            act.wait_ge(s["state_stored"], 48)
            for b in range(NB):
                nc.scalar.activation(hTh1[:, :, b * P:b * P + P], ps[:, 2 * b:2 * b + 2, :].rearrange("p a (c n) -> p (a c) n", n=P),
                                     ACT.Copy).then_inc(s["yT_hi"], 1)
            for n in range(WOUT + SPLIT, FFN + 2):
                split_hi(act, n, n, n // RAW + 1)
            save_gate(0)
            norm(1)
            modulate(1, 1, hTf1, hTh1)

            def ffn_split(n, k, turn, count):
                for i in range(count):
                    split_hi(act, n + i, k + i, turn + (k + i) // RAW + 1)

            def ffn_silu(n_gate):
                act.wait_ge(s["weights_used"], used(n_gate))
                for b in range(NB):
                    nc.scalar.activation(sg[:, b], ps[:, 2 * b, :], ACT.Silu).then_inc(s["silu_ready"], 1)

            def ffn_boundary(n, k, turn, c):
                ffn_split(n, k, turn, 3)
                for b in range(NB):
                    act.wait_ge(s["h_turned"], NB * c + b + 1)
                    nc.scalar.activation(hcTh[:, :, b * P:b * P + P], ps[:, 2 * b, :].rearrange("p (t n) -> p t n", n=P),
                                         ACT.Copy).then_inc(s["hc_hi"], 1)
                ffn_split(n + 3, k + 3, turn, 1)
                copy_row(n + 1, m41, 0, 3)

            ffn_split(FFN + 2, FFN + 2, 0, 2)
            ffn_silu(FFN + 1)
            ffn_boundary(FFN + 4, FFN + 4, 0, 0)
            with act.Fori(0, (NC - 1) // UNROLL) as r:
                for u in range(UNROLL):
                    k = ffn_unit(u)
                    n = k + FFN_CHUNK * UNROLL * r
                    turn = FFN_CHUNK * UNROLL // RAW * r
                    ffn_split(n, k, turn, 2)
                    copy_row(n - 1, m41, 1, 1)
                    ffn_split(n + 2, k + 2, turn, 2)
                    ffn_silu(n + 1)
                    ffn_split(n + 4, k + 4, turn, 2)
                    ffn_boundary(n + 6, k + 6, turn, UNROLL * r + u + 1)
            ffn_split(MOE - 2, MOE - 2, 0, 2)
            copy_row(MOE - 3, m41, 1, 1)
            save_gate(1)
            norm(2)
            fetch(poolw[:, :, :], pool_w[0].rearrange("g (t p) n -> p (g t) n", p=P), "poolw_loaded")
            save_gate(2)
            norm(3)
            fetch(w_rt[:, :, :], w_router[0].rearrange("(t p) e -> p t e", p=P), "poolw_loaded")
            modulate(2, 3, hTf1)
            for b in range(NB):
                act.wait_ge(s["htok_turned"], b + 1)
                nc.scalar.activation(htok_h[:, b], ps[:, 4 + 2 * b:6 + 2 * b, :], ACT.Copy).then_inc(s["htok_hi"], 1)
            act.wait_ge(s["route_dd"], 1)
            nc.scalar.activation(rt[:, 5, :, 1:2], rt[:, 5, :, 0:1], ACT.Exp).then_inc(s["route_exp"], 1)

            def save_gathered(q, cnt):
                act.wait_ge(s["gathered_hi"], cnt)
                nc.scalar.activation(hTh1[:, :, q * P:q * P + P].rearrange("p (a c) n -> p a c n", c=4),
                                     ps[:, 6:8, :].rearrange("p a (c n) -> p a c n", n=P), ACT.Copy).then_inc(s["xg_hi"], 1)

            def save_result(n_last):
                act.wait_ge(s["weights_used"], used(n_last))
                nc.scalar.activation(yh.rearrange("p (a n) -> p a n", n=512), ps[:, 2:4, :], ACT.Copy).then_inc(s["y_hi"], 1)

            def expert(n0, turn0, hbase, q, j):
                def save_hidden(cnt):
                    act.wait_ge(s["h_turned"], cnt + 1)
                    nc.scalar.activation(hcTh[:, :, 0:P], ps[:, 4, :].rearrange("p (t n) -> p t n", n=P), ACT.Copy)\
                        .then_inc(s["hc_hi"], 1)

                def gate_silu(n_gate):
                    act.wait_ge(s["weights_used"], used(n_gate))
                    nc.scalar.activation(sg[:, 0], ps[:, 0, :], ACT.Silu).then_inc(s["silu_ready"], 1)

                def chunk(cc, peeled):
                    m = n0 + 6 * cc - 2
                    for k in range(6):
                        if k == 2:
                            save_hidden(hbase + cc - 1)
                            if peeled == 2:
                                save_gathered(1 - q, j + 2)
                        split_hi(act, m + k, 4 + k, turn0 + cc + (4 + k) // RAW)
                        if k == 3:
                            gate_silu(m + 1)

                for k in range(4):
                    split_hi(act, n0 + k, k, turn0 + 1)
                    if k == 1:
                        save_result(n0 - 1)
                gate_silu(n0 + 1)
                chunk(1, 1)
                chunk(2, 2)
                with act.Fori(3, NC) as cc:
                    chunk(cc, 0)
                split_hi(act, n0 + UNITS_E - 2, 4, turn0 + NC)
                save_hidden(hbase + NC - 1)
                split_hi(act, n0 + UNITS_E - 1, 5, turn0 + NC)

            act.wait_ge(s["npass_ready"], 1)
            passes = nc.scalar.value_load(npass[0:1, 0:1], min_val=1, max_val=2)
            save_gate(3)
            fetch(finalg, final_g.partition_broadcast(P), "finalg_loaded")
            save_gathered(0, 1)
            act.wait_ge(s["result_zeroed"], 1)
            with act.Fori(0, passes) as p:
                with act.Fori(0, N_EXP // 2) as e2:
                    for q in range(2):
                        j = p * N_EXP + e2 * 2 + q
                        expert(MOE + UNITS_E * j, MOE // RAW + NC * j, NB * NC + NC * j, q, j)
            save_result(MOE + UNITS_E * N_EXP * passes - 1)
            norm(4)

        @block.vector
        def _(dve):
            steps = [0]
            VT = nc.vector.tensor_tensor

            def step(ins):
                steps[0] += 1
                ins.then_inc(s["dve_step"], 1)
                dve.wait_ge(s["dve_step"], steps[0])

            dve.wait_ge(s["rows_turned"], 2)
            dve.wait_ge(s["csil_ready"], 1)
            nc.vector.tensor_copy(cols[:, :], ps[:, 7, 0:92])
            step(nc.vector.tensor_copy(flat(bcol), ps[:, 6, 128:224]))
            nc.vector.memset(csp[:, :, :].bitcast(F32), 0.0).then_inc(s["cols_saved"], 1)
            dve.wait_ge(s["csil_ready"], 1)
            dve.wait_ge(s["cols_saved"], 1)
            def split_conditions(c):
                cs = csil.rearrange("p (b k) -> p k b", b=NB)
                step(nc.vector.tensor_copy(c[:, :, 0:2], cs))
                VT(c[:, :, 2:4], cs, c[:, :, 0:2].bitcast(F32), ALU.subtract).then_inc(s["csplit_ready"], 1)
            split_conditions(csp)

            mcol_all = mcol.rearrange("p l k b -> p (l k) b")

            def save_cols(count, bank, f, chunks=1):
                dve.wait_ge(s["mod_cols_turned"], count + 1)
                VT(mcol_all[:, bass.ds(4 * f, 4 * chunks), :],
                   ps[:, bank, 0:8 * chunks].rearrange("p (k b) -> p k b", b=NB),
                   rep(flat(bcol)[:, bass.ds(4 * f, 4 * chunks)], 2, NB), ALU.add).then_inc(s["mod_cols_saved"], 1)

            def scales(i, saved):
                dve.wait_ge(s["mod_cols_saved"], saved)
                c = 24 * (i % 2) + 8
                step(nc.vector.scalar_tensor_tensor(scp[:, i], mcol[:, i // 2, c:c + 8], 1.0,
                                                    rep(ng_cols[:, i], 2, NB), ALU.add, ALU.mult))

            def norm(i, normalise=True):
                xn = xn0 if i == 0 else xn1
                dve.wait_ge(s["sumsq_ready"], 2 * i + 2)
                nc.vector.tensor_scalar(var[:, :], sumsq[:, :], 1.0 / D, EPS, ALU.mult, ALU.add).then_inc(s["var_ready"], 1)
                dve.wait_ge(s["std_ready"], i + 1)
                step(nc.vector.reciprocal(rstd[:, :], std[:, :]))
                if normalise:
                    for b in range(NB):
                        nc.vector.tensor_scalar(xn[:, b], x[:, b], rstd[:, b:b + 1], None, ALU.mult).then_inc(s["xn_ready"], 1)

            def modulate(m, i, hTf, hTh=None, hTl=None):
                for b in range(NB):
                    dve.wait_ge(s["xn_turned"], 2 * m + b + 1)
                    for t in range(4):
                        last = nc.vector.tensor_scalar(hTf[:, t, b * P:b * P + P], ps[:, 4 + 2 * b, t * P:t * P + P],
                                                       scp[:, i, t, b:b + 1], mcol[:, i // 2, 24 * (i % 2) + t, b:b + 1],
                                                       ALU.mult, ALU.add)
                    last.then_inc(s["hT_by_vector"], 1)
                for b in range(NB if hTh is not None else 0):
                    dve.wait_ge(s["h_hi_ready"], 2 * m + b + 1)
                    VT(hTl[:, :, b * P:b * P + P], hTf[:, :, b * P:b * P + P], hTh[:, :, b * P:b * P + P].bitcast(F32),
                       ALU.subtract).then_inc(s["h_lo_ready"], 1)

            for f in range(MOD_FIRST + 1):
                for h in range(2 if f < MOD_FIRST else 0):
                    split_lo(dve, mod_unit(f, h), mod_unit(f, h))
                if f >= 2:
                    save_cols(f - 2, 3, f - 2)
            save_cols(MOD_FIRST - 1, 3, MOD_FIRST - 1)
            scales(0, MOD_FIRST)
            dve.sem_inc(s["scp_ready"], 1)
            norm(0)
            modulate(0, 0, hTf0, hTh0, hTl0)
            dve.wait_ge(s["ab_turned"], 1)
            nc.vector.tensor_copy(ab.rearrange("p b n -> p (b n)"), ps[:, 7, 0:32]).then_inc(s["ab_saved"], 1)
            for i in range(len(WIN_ORDER)):
                f = MOD_FIRST + i
                split_lo(dve, win_unit(i), win_unit(i))
                if i >= 2:
                    save_cols(f - 2, 3, f - 2)
                split_lo(dve, win_unit(i, 1), win_unit(i, 1))
                for h in range(2 if i < MOD_WIN else 0):
                    split_lo(dve, mod_unit(f, h), mod_unit(f, h))
            save_cols(MOD_FFN - 1, 3, MOD_FFN - 1)
            scales(1, MOD_FFN)

            def col(i):
                return sm[:, i]
            dve.wait_ge(s["small_loaded"], 64)
            step(VT(col(0).rearrange("p (b n) -> p b n", b=NB), ab[:, :, 0:8], rep(dtb[:, :], 1, NB), ALU.add))
            nc.vector.tensor_scalar(col(2), col(0), 0.0, None, ALU.max)
            nc.vector.scalar_tensor_tensor(col(1), col(0), -1.0, col(0), ALU.mult, ALU.max).then_inc(s["soft_in"], 1)
            dve.wait_ge(s["softplus_l"], 1)
            dve.wait_ge(s["soft_in"], 1)
            nc.vector.tensor_scalar(col(9), col(6), 0.5, 0.5, ALU.mult, ALU.add).then_inc(s["beta_ready"], 1)
            step(VT(col(7), col(2), col(4), ALU.add))
            nc.vector.scalar_tensor_tensor(col(8).rearrange("p (b n) -> p b n", b=NB), col(7).rearrange("p (b n) -> p b n", b=NB),
                                           -1.0, rep(sm[:, 5, 0:8], 1, NB), ALU.mult, ALU.mult).then_inc(s["g_ready"], 1)
            def conv_tmp(t):
                return (LT if t < 8 else CTa)[:, 2 * (t % 8):2 * (t % 8) + 2]
            for tap in (0, 2):
                for t in range(12):
                    if tap == 0:
                        dve.wait_ge(s["conv_mid"], t + 1)
                    elif t == 0:
                        dve.wait_ge(s["conv_sum"], 12)
                    src = b_ch[:, t].rearrange("p (b n) -> p b n", b=NB)
                    dst, src = ((conv_tmp(t)[:, :, 1:P], src[:, :, 0:P - 1]) if tap == 0 else
                                (conv_tmp(t)[:, :, 0:P - 1], src[:, :, 1:P]))
                    nc.vector.scalar_tensor_tensor(dst, src, conv_cols[:, tap, t:t + 1], dst, ALU.mult, ALU.add)\
                        .then_inc(s["conv_sum"], 1)
            dve.wait_ge(s["gc_turned"], 1)
            step(nc.vector.tensor_copy(col(10), ps[:, 6, 0:16]))
            VT(col(11), ps[:, 6, 16:32], col(10), ALU.subtract).then_inc(s["gc_saved"], 1)
            for b in range(NB):
                dve.wait_ge(s["gcrow_turned"], b + 1)
                for d in range(2):
                    cut = slice(8 * b + 4 * d, 8 * b + 4 * d + 4)
                    last = VT(decay[:, cut], ps[:, 6 + d].rearrange("p (h n) -> p h n", n=P),
                              rep(sm[:, 10, cut], 2, P), ALU.subtract)
                step(last)
                nc.vector.tensor_scalar(decay[:, 8 * b:8 * b + 8], decay[:, 8 * b:8 * b + 8], 0.0, None, ALU.max)\
                    .then_inc(s["diff_ready"], 1)
            PR = (X[:, 0:8], X[:, 8:16], XT[:, 0:8])
            mx = sm[:, 18:21].rearrange("p a (c n) -> p (a c) n", n=8)
            den = sm[:, 21:23].rearrange("p a (c n) -> p (a c) n", n=8)
            dve.wait_ge(s["bias_masked"], 1)
            for i in range(3):
                dve.wait_ge(s["scores_turned"], i + 1)
                nc.vector.tensor_reduce(mx[:, i], ps[:, 2 * i:2 * i + 2, :].rearrange("p a (c n) -> p (a c) n", n=P),
                                        AX.X, ALU.max).then_inc(s["mx_ready"], 1)
            dve.wait_ge(s["mx_ready"], 3)
            step(VT(mx[:, 3], mx[:, 1], mx[:, 2], ALU.max))
            for i in range(3):
                VT(PR[i], ps[:, 2 * i:2 * i + 2, :].rearrange("p a (c n) -> p (a c) n", n=P),
                   rep(mx[:, 0 if i == 0 else 3], 2, P), ALU.subtract).then_inc(s["p_in"], 1)
            dve.wait_ge(s["rq_ready"], 1)
            nc.vector.reciprocal(sm[:, 17], sm[:, 16]).then_inc(s["len_inverse"], 1)
            dve.wait_ge(s["len_inverse"], 1)
            VT(LT[:, 8:16], rep(ident[:, :], 1, 8), rep(sm[:, 17, 8:16], 2, P), ALU.mult).then_inc(s["len_diag"], 1)
            for i in range(3):
                dve.wait_ge(s["p_exp"], i + 1)
                last = nc.vector.tensor_reduce(den[:, i], PR[i], AX.X, ALU.add)
            step(last)
            step(VT(den[:, 1], den[:, 1], den[:, 2], ALU.add))
            step(nc.vector.reciprocal(den[:, 0:2], den[:, 0:2]))
            dve.wait_ge(s["len_turned"], 1)
            qv = b_ch[:, 0:4].rearrange("p a (c n) -> p (a c) n", n=P)
            kv = b_ch[:, 4:8].rearrange("p a (c n) -> p (a c) n", n=P)
            inv = ps[:, 4:8, :].rearrange("p a (c n) -> p (a c) n", n=P)
            VT(kv, kv, inv[:, 8:16], ALU.mult).then_inc(s["kn_ready"], 1)
            nc.vector.scalar_tensor_tensor(qv, qv, DK ** -0.5, inv[:, 0:8], ALU.mult, ALU.mult).then_inc(s["qn_ready"], 1)
            for b in range(NB):
                dve.wait_ge(s["o_turned"], b + 1)
                for par in range(2):
                    last = VT(y[:, b, 0:512].rearrange("p (a r n) -> p a r n", r=2, n=DH_A)[:, :, par],
                              ps[:, b].rearrange("p (a r n) -> p a r n", r=2, n=DH_A)[:, :, par],
                              rep(den[:, b, 4 * par:4 * par + 4], 2, DH_A), ALU.mult)
                last.then_inc(s["oa_ready"], 1)
            def bank(i):
                return ps[:, i].rearrange("p (h n) -> p h n", n=P)
            for n in range(WOUT, WOUT + 2):
                split_lo(dve, n, n)
            for b in range(NB):
                dve.wait_ge(s["qk_turned"], b + 1)
                dve.wait_ge(s["decay_ready"], b + 1)
                for d in range(2):
                    cut = slice(8 * b + 4 * d, 8 * b + 4 * d + 4)
                    last = VT(attn[:, cut], bank(2 + b), decay[:, cut], ALU.mult)
                step(last)
                for d in range(2):
                    cut = slice(8 * b + 4 * d, 8 * b + 4 * d + 4)
                    last = VT(decay[:, cut], bank(b), decay[:, cut], ALU.mult)
                step(last)
                VT(decay[:, 8 * b:8 * b + 8], decay[:, 8 * b:8 * b + 8], rep(sm[:, 9, 8 * b:8 * b + 8], 2, P), ALU.mult)\
                    .then_inc(s["L_beta"], 1)
                dve.wait_ge(s["L_beta"], b + 1)
                dve.wait_ge(s["tri_ready"], 1)
                v = decay[:, 8 * b:8 * b + 8].rearrange("p (d h) n -> p d h n", d=2)
                VT(v, v, rep(tri[:, 2:4], 2, H_B), ALU.mult).then_inc(s["L_masked"], 1)
            dve.wait_ge(s["L_masked"], 2)
            for g in range(4):
                cut = slice(4 * g, 4 * g + 4)
                last = VT(X[:, cut], decay[:, cut], rep(lev[:, 0, 1 - g % 2], 1, 4), ALU.mult)
            last.then_inc(s["x1_tmp"], 1)
            dve.wait_ge(s["v_turned"], 1)
            dve.wait_ge(s["beta_ready"], 1)
            dve.wait_ge(s["gc_saved"], 1)
            for d in range(2):
                VT(R[:, 4 * d:4 * d + 4], bank(4), rep(sm[:, 9, 4 * d:4 * d + 4], 2, P), ALU.mult)
            dve.wait_ge(s["ks_turned"], 1)
            dve.wait_ge(s["egc_ready"], 1)
            for d in range(2):
                last = VT(R[:, 8 + 4 * d:12 + 4 * d], bank(6 + d), rep(sm[:, 12, 8 + 4 * d:12 + 4 * d], 2, P), ALU.mult)
            step(last)
            for d in range(2):
                last = VT(R[:, 8 + 4 * d:12 + 4 * d], bank(5), R[:, 8 + 4 * d:12 + 4 * d], ALU.subtract)
            step(last)
            VT(R[:, 8:16], R[:, 8:16], rep(sm[:, 9, 8:16], 2, P), ALU.mult).then_inc(s["rhs_ready"], 1)
            dve.wait_ge(s["LT_saved"], 1)
            for g in range(4):
                cut = slice(4 * g, 4 * g + 4)
                last = VT(XT[:, cut], LT[:, cut], rep(lev[:, 0, g % 2], 1, 4), ALU.mult)
            step(last)
            for g in range(4):
                cut = slice(4 * g, 4 * g + 4)
                VT(X[:, cut], rep(ident[:, :], 1, 4), X[:, cut], ALU.subtract)
                VT(XT[:, cut], rep(ident[:, :], 1, 4), XT[:, cut], ALU.subtract).then_inc(s["xx_saved"], 1)
            with dve.Fori(0, LEVELS - 1) as l:
                dve.wait_ge(s["xx_saved"], 4 * l + 4)
                for g in range(4):
                    cut = slice(4 * g, 4 * g + 4)
                    dve.wait_ge(s["xx_turned"], 4 * l + g + 1)
                    VT(X[:, cut], X[:, cut], bank(4 + 2 * (g % 2)), ALU.subtract)
                    VT(XT[:, cut], XT[:, cut], bank(5 + 2 * (g % 2)), ALU.subtract).then_inc(s["xx_saved"], 1)
            split_lo(dve, WOUT + 2, WOUT + 2)
            dve.wait_ge(s["qs_turned"], 1)
            for d in range(2):
                last = VT(R[:, 4 * d:4 * d + 4], bank(6 + d), rep(sm[:, 12, 8 + 4 * d:12 + 4 * d], 2, P), ALU.mult)
            step(last)
            yb1 = y[:, 1, 512:1024].rearrange("p (h n) -> p h n", n=P)
            step(VT(yb1, bank(5), R[:, 0:4], ALU.add))
            step(VT(yb1, yb1, R[:, 4:8], ALU.add))
            dve.wait_ge(s["ob0_ready"], 1)
            for b in range(NB):
                yb = y[:, b, 512:1024].rearrange("p (h n) -> p h n", n=P)
                last = VT(R[:, 8 + 4 * b:12 + 4 * b], yb, yb, ALU.mult)
            step(last)
            step(nc.vector.tensor_reduce(sm[:, 14, 0:8], R[:, 8:16], AX.X, ALU.add))
            nc.vector.tensor_scalar(sm[:, 15, 0:8], sm[:, 14, 0:8], 1.0 / DK, EPS, ALU.mult, ALU.add).then_inc(s["yss_ready"], 1)
            dve.wait_ge(s["ystd_ready"], 1)
            dve.wait_ge(s["z_gained"], 1)
            step(nc.vector.reciprocal(sm[:, 17, 0:8], sm[:, 16, 0:8]))
            for b in range(NB):
                yb = y[:, b, 512:1024].rearrange("p (h n) -> p h n", n=P)
                last = VT(yb, yb, rep(sm[:, 17, 4 * b:4 * b + 4], 2, P), ALU.mult)
            step(last)
            VT(y[:, :, 512:1024], y[:, :, 512:1024], z[:, :, :], ALU.mult).then_inc(s["yb_ready"], 1)

            for b in range(NB):
                dve.wait_ge(s["yT_hi"], b + 1)
                VT(hTl1[:, :, b * P:b * P + P], ps[:, 2 * b:2 * b + 2, :].rearrange("p a (c n) -> p (a c) n", n=P),
                   hTh1[:, :, b * P:b * P + P].bitcast(F32), ALU.subtract).then_inc(s["yT_lo"], 1)
            for n in range(WOUT + SPLIT, FFN + 2):
                split_lo(dve, n, n)
            step(nc.vector.memset(csp1.bitcast(F32), 0.0))
            split_conditions(csp1)

            def update(i, n_last):
                dve.wait_ge(s["gates_saved"], i + 1)
                if n_last is not None:
                    dve.wait_ge(s["weights_used"], used(n_last))
                for b in range(NB):
                    for h in range(2):
                        last = VT(tmp[:, h], ps[:, 4 + 2 * b + h, :], gate_bc[:, b, 512 * h:512 * h + 512], ALU.mult)
                    step(last)
                    xb = x[:, b].rearrange("p (h n) -> p h n", n=512)
                    step(VT(xb, xb, tmp[:, :, :], ALU.add))
                dve.sem_inc(s["x_updated"], 1)

            update(0, FFN - 1)
            norm(1)
            modulate(1, 1, hTf1, hTh1, hTl1)

            def ffn_lo(n, k, count):
                for i in range(count):
                    split_lo(dve, n + i, k + i)

            def ffn_hidden(n_up, c):
                dve.wait_ge(s["weights_used"], used(n_up))
                for b in range(NB):
                    dve.wait_ge(s["silu_ready"], NB * c + b + 1)
                    VT(hc[:, b], sg[:, b], ps[:, 2 * b + 1, :], ALU.mult).then_inc(s["h_ready"], 1)

            def ffn_boundary(n, k, c, first=False):
                ffn_lo(n, k, 2)
                if not first:
                    save_cols(MOD_FFN + c - 1, 1, MOD_FFN + 2 * (c - 1), 2)
                for b in range(NB):
                    dve.wait_ge(s["hc_hi"], NB * c + b + 1)
                    VT(hcTl[:, :, b * P:b * P + P], ps[:, 2 * b, :].rearrange("p (t n) -> p t n", n=P),
                       hcTh[:, :, b * P:b * P + P].bitcast(F32), ALU.subtract).then_inc(s["hc_lo"], 1)
                ffn_lo(n + 2, k + 2, 2)

            ffn_lo(FFN + 2, FFN + 2, 2)
            ffn_hidden(FFN + 3, 0)
            ffn_boundary(FFN + 4, FFN + 4, 0, first=True)
            with dve.Fori(0, (NC - 1) // UNROLL) as r:
                for u in range(UNROLL):
                    k = ffn_unit(u)
                    n = k + FFN_CHUNK * UNROLL * r
                    ffn_lo(n, k, 6)
                    ffn_hidden(n + 3, UNROLL * r + u + 1)
                    ffn_boundary(n + 6, k + 6, UNROLL * r + u + 1)
            ffn_lo(MOE - 2, MOE - 2, 2)
            update(1, MOE - 1)
            save_cols(MOD_FFN + NC - 1, 1, 22, 2)
            scales(2, MOD_FFN + NC)
            scales(3, MOD_FFN + NC)
            VT(pgate[:, :, :], mcol[:, 1, 16:24], rep(pscale_cols, 2, NB), ALU.mult).then_inc(s["pgate_ready"], 1)
            dve.wait_ge(s["counts_turned"], 1)
            step(nc.vector.reciprocal(tmp[:, 0], ps[:, 3]))
            step(VT(flat(band), flat(band), tmp[:, 0], ALU.mult))
            VT(band[:, :, :], band[:, :, :], rep(ident[:, :], 1, 4), ALU.subtract).then_inc(s["band_scaled"], 1)
            norm(2)
            for b in range(NB):
                dve.wait_ge(s["pooled"], b + 1)
                VT(hTf1[:, :, b * P:b * P + P], ps[:, 2 * b:2 * b + 2, :].rearrange("p a (c n) -> p (a c) n", n=P),
                   rep(scp[:, 2, :, b], 2, P), ALU.mult).then_inc(s["yp_ready"], 1)
            dve.wait_ge(s["pool_mixed"], 1)
            update(2, None)
            norm(3)
            modulate(2, 3, hTf1)
            dve.wait_ge(s["logits_turned"], 1)
            step(nc.vector.tensor_copy(rt[:, 0].rearrange("p b e -> p (b e)"), ps[:, 0, 0:16]))
            for b in range(NB):
                last = nc.vector.max(rt[:, 1, b], rt[:, 0, b])
            step(last)
            for b in range(NB):
                last = nc.vector.max_index(idx8[:, b], rt[:, 1, b], rt[:, 0, b])
            step(last)
            VT(rt[:, 5, :, 0:1], rt[:, 1, :, 1:2], rt[:, 1, :, 0:1], ALU.subtract).then_inc(s["route_dd"], 1)
            step(nc.vector.tensor_copy(rt[:, 2], idx8[:, :, :]))
            for i in range(2):
                last = VT(rt[:, 3 + i], rep(iota[:, 0:N_EXP], 1, NB), rt[:, 2, :, i:i + 1].broadcast_to([P, NB, N_EXP]), ALU.is_equal)
            step(last)
            step(VT(rt[:, 7], rt[:, 3], rt[:, 4], ALU.add))
            dve.sem_inc(s["mask_ready"], 1)
            dve.wait_ge(s["route_exp"], 1)
            step(nc.vector.tensor_scalar(rt[:, 5, :, 2:3], rt[:, 5, :, 1:2], 1.0, None, ALU.add))
            step(nc.vector.reciprocal(rt[:, 5, :, 3:4], rt[:, 5, :, 2:3]))
            step(VT(rt[:, 5, :, 4:5], rt[:, 5, :, 3:4], rt[:, 5, :, 1:2], ALU.mult))
            for i in range(2):
                last = VT(rt[:, 8 + i], rt[:, 3 + i], rt[:, 5, :, 3 + i:4 + i].broadcast_to([P, NB, N_EXP]), ALU.mult)
            step(last)
            step(VT(rt[:, 10], rt[:, 8], rt[:, 9], ALU.add))
            dve.wait_ge(s["pos_turned"], 1)
            step(nc.vector.scalar_tensor_tensor(rt[:, 11].rearrange("p b e -> p (b e)"), ps[:, 1, 0:16], 1.0,
                                                rt[:, 7].rearrange("p b e -> p (b e)"), ALU.add, ALU.mult))
            for q in range(NB):
                cut = slice(N_EXP * q, N_EXP * q + N_EXP)
                nc.vector.tensor_scalar(posj[:, cut].rearrange("p e b -> p b e"), rt[:, 11], -1.0 - P * q, None, ALU.add)
                nc.vector.tensor_copy(gatej[:, cut].rearrange("p e b -> p b e"), rt[:, 10])
            step(nc.vector.tensor_reduce(rt[:, 12, 0, 0:1], ps[:, 1, 16:24], AX.X, ALU.max))
            nc.vector.tensor_scalar(npass[:, :], rt[:, 12, 0, 0:1], float(P), 1.0, ALU.is_gt, ALU.add).then_inc(s["npass_ready"], 1)
            for b in range(NB):
                dve.wait_ge(s["htok_hi"], b + 1)
                VT(htok_l[:, b], ps[:, 4 + 2 * b:6 + 2 * b, :].rearrange("p a n -> p (a n)"), htok_h[:, b].bitcast(F32),
                   ALU.subtract).then_inc(s["htok_lo"], 1)

            def slots(j):
                VT(ST[:, :, :], rep(iota[:, :], 1, NB), posj[:, j, :].unsqueeze(2).broadcast_to([P, NB, P]),
                   ALU.is_equal).then_inc(s["st_ready"], 1)

            def save_gathered(q, cnt):
                dve.wait_ge(s["gathered_lo"], cnt)
                nc.vector.tensor_copy(hTl1[:, :, q * P:q * P + P].rearrange("p (a c) n -> p a c n", c=4),
                                      ps[:, 6:8, :].rearrange("p a (c n) -> p a c n", n=P)).then_inc(s["xg_lo"], 1)

            def save_result(cnt):
                dve.wait_ge(s["y_hi"], cnt)
                VT(yl.rearrange("p (a n) -> p a n", n=512), ps[:, 2:4, :],
                   yh.rearrange("p (a n) -> p a n", n=512).bitcast(F32), ALU.subtract).then_inc(s["y_lo"], 1)

            def collect(b, cnt):
                dve.wait_ge(s["scattered"], cnt)
                out = acc[:, b].rearrange("p (h n) -> p h n", n=512)
                nc.vector.scalar_tensor_tensor(out, ps[:, 6:8, :], gcur[:, b:b + 1], out, ALU.mult, ALU.add)\
                    .then_inc(s["acc_added"], 1)

            def expert(n0, hbase, q, j):
                def save_hidden(cnt):
                    dve.wait_ge(s["hc_hi"], cnt + 1)
                    VT(hcTl[:, :, 0:P], ps[:, 4, :].rearrange("p (t n) -> p t n", n=P),
                       hcTh[:, :, 0:P].bitcast(F32), ALU.subtract).then_inc(s["hc_lo"], 1)

                def hidden(n_up, cnt):
                    dve.wait_ge(s["weights_used"], used(n_up))
                    dve.wait_ge(s["silu_ready"], cnt + 1)
                    VT(hc[:, 0], sg[:, 0], ps[:, 1, :], ALU.mult).then_inc(s["h_ready"], 1)

                def chunk(cc, peeled):
                    m = n0 + 6 * cc - 2
                    for k in range(6):
                        if k == 2:
                            save_hidden(hbase + cc - 1)
                            if peeled == 1:
                                collect(0, 2 * j + 1)
                        if k == 4 and peeled == 1:
                            collect(1, 2 * j + 2)
                            dve.wait_ge(s["acc_added"], 2 * j + 2)
                            nc.vector.tensor_copy(Sm.rearrange("p b n -> p (b n)"), ps[:, 5, 0:NB * P])
                            nc.vector.tensor_copy(gcur[:, :], gatej[:, j, :]).then_inc(s["s_saved"], 1)
                        if k == 4 and peeled == 2:
                            save_gathered(1 - q, j + 2)
                        if not (peeled == 1 and k == 0):
                            split_lo(dve, m + k, 4 + k)
                    hidden(m + 3, hbase + cc)

                for k in range(4):
                    split_lo(dve, n0 + k, k)
                    if k == 1:
                        save_result(j + 1)
                        slots(j + 1)
                split_lo(dve, n0 + 4, 4)
                hidden(n0 + 3, hbase)
                chunk(1, 1)
                chunk(2, 2)
                with dve.Fori(3, NC) as cc:
                    chunk(cc, 0)
                split_lo(dve, n0 + UNITS_E - 2, 4)
                save_hidden(hbase + NC - 1)
                split_lo(dve, n0 + UNITS_E - 1, 5)

            dve.wait_ge(s["npass_ready"], 1)
            passes = nc.vector.value_load(npass[0:1, 0:1], min_val=1, max_val=2)
            dve.wait_ge(s["acc_zeroed"], 1)
            slots(0)
            save_gathered(0, 1)
            with dve.Fori(0, passes) as p:
                with dve.Fori(0, N_EXP // 2) as e2:
                    for q in range(2):
                        j = p * N_EXP + e2 * 2 + q
                        expert(MOE + UNITS_E * j, NB * NC + NC * j, q, j)
            save_result(passes * N_EXP + 1)
            collect(0, passes * (2 * N_EXP) + 1)
            collect(1, passes * (2 * N_EXP) + 2)
            dve.wait_ge(s["acc_added"], passes * (2 * N_EXP) + 2)
            dve.wait_ge(s["gates_saved"], 4)
            for b in range(NB):
                step(VT(acc[:, b], acc[:, b], gate_bc[:, b], ALU.mult))
                step(VT(x[:, b], x[:, b], acc[:, b], ALU.add))
            dve.sem_inc(s["x_updated"], 1)
            norm(4, normalise=False)
            dve.wait_ge(s["finalg_loaded"], 16)
            for b in range(NB):
                last = nc.vector.scalar_tensor_tensor(xn1[:, b], x[:, b], rstd[:, b:b + 1], finalg, ALU.mult, ALU.mult)
            last.then_inc(s["y_ready"], 1)

        @block.tensor
        def _(pe):
            MM = nc.tensor.matmul

            def turn(out, src, n=P):
                return nc.tensor.transpose(out, src, ident[0:n, 0:n])

            pe.sem_inc(s["weights_used"], SPLIT)
            pe.wait_ge(s["consts_ready"], 1)
            pe.wait_ge(s["rows_loaded"], 96)
            turn(ps[:, 7, 0:92], rowsA[0:92, :], 92).then_inc(s["rows_turned"], 1)
            turn(ps[:, 6, 128:224], rowsB[0:96, :], 96).then_inc(s["rows_turned"], 1)

            def mod_product(n, k, c, bank):
                for h in range(2):
                    pe.wait_ge(s["lo_ready"], n + h + 1)
                    for t in range(4):
                        MM(ps[:, bank, :], c[:, 4 * h + t, :], w_hi[:, (k + h) % SPLIT, t, :], start=h == 0 and t == 0, stop=False)
                        last = MM(ps[:, bank, :], c[:, 4 * h + t, :], w_lo[:, (k + h) % SPLIT, t, :], start=False,
                                  stop=h == 1 and t == 3)
                    last.then_inc(s["weights_used"], 1)

            def mod_cols(m, slots, bank):
                for i, j in enumerate(slots):
                    for t in range(4):
                        o = 2 * (4 * i + t)
                        last = MM(ps[:, bank, o:o + 2], m[0:4, j, t * P:t * P + P], fold[0:4, :], start=True, stop=True)
                last.then_inc(s["mod_cols_turned"], 1)

            def turn_xn(m, nidx, xn):
                for b in range(NB):
                    pe.wait_ge(s["xn_ready"], 2 * nidx + b + 1)
                    for t in range(KT):
                        last = turn(ps[:, 4 + 2 * b + t // 4, (t % 4) * P:(t % 4 + 1) * P], xn[:, b, t * P:t * P + P])
                    last.then_inc(s["xn_turned"], 1)

            pe.wait_ge(s["csplit_ready"], 1)
            for f in range(MOD_FIRST + 1):
                if f < MOD_FIRST:
                    if f == 3:
                        pe.wait_ge(s["mod_rows_copied"], 1)
                    mod_product(mod_unit(f), mod_unit(f), csp, f % 3)
                if f:
                    pe.wait_ge(s["mod_rows_copied"], f)
                    if f >= 2:
                        pe.wait_ge(s["mod_cols_saved"], f - 1)
                    mod_cols(m4, [(f - 1) % 3], 3)
            turn_xn(0, 0, xn0)

            pe.wait_ge(s["h_lo_ready"], 2)
            pe.wait_ge(s["small_loaded"], 64)
            for b in range(NB):
                for t in range(KT):
                    last = MM(ps[:, 7, 16 * b:16 * b + 16], hTf0[:, t, b * P:b * P + P], w_ab[:, t, :], start=t == 0, stop=t == KT - 1)
            last.then_inc(s["ab_turned"], 1)
            for i, (kind, _) in enumerate(WIN_ORDER):
                b0 = 4 * (i % 2)
                if i == 1:
                    pe.wait_ge(s["ab_saved"], 1)
                if i >= 2:
                    pe.wait_ge(s["proj_saved"], i - 1)
                for h in range(2):
                    n = win_unit(i, h)
                    if kind in ("av", "z"):
                        multiply(pe, n, n, hTh0, hTl0, 4 * h, [(0, b0), (1, b0 + 1)], h == 0, h == 1)
                        continue
                    pe.wait_ge(s["lo_ready"], n + 1)
                    for bank in (b0, b0 + 1) if h == 0 else ():
                        MM(ps[:, bank, :].rearrange("p (k n) -> p k n", n=64), csp[:, 0, :], csp[:, :, 64:P],
                           start=True, stop=False)
                    for q in range(4):
                        out = ps[:, b0 + q // 2, (q % 2) * 256:(q % 2 + 1) * 256]
                        for t in range(4):
                            kt = 4 * h + t
                            wh = w_hi[:, n % SPLIT, t, q * P:q * P + P]
                            MM(out, wh, hTh0[:, kt, :], start=False, stop=False)
                            MM(out, wh, hTl0[:, kt, :], start=False, stop=False)
                            last = MM(out, w_lo[:, n % SPLIT, t, q * P:q * P + P], hTh0[:, kt, :], start=False,
                                      stop=kt == KT - 1 and q % 2 == 1)
                    last.then_inc(s["weights_used"], 1)
                f = MOD_FIRST + i
                if i:
                    pe.wait_ge(s["mod_rows_copied"], f)
                if i < MOD_WIN:
                    mod_product(mod_unit(f), mod_unit(f), csp, 2)
                if i:
                    pe.wait_ge(s["mod_cols_saved"], f - 1)
                    mod_cols(m4, [(f - 1) % 3], 3)
            pe.wait_ge(s["proj_saved"], 7)
            pe.wait_ge(s["mod_cols_saved"], MOD_FFN)

            pe.wait_ge(s["cache_loaded"], 48)
            for i in range(4):
                turn(ps[:, 4, i * P:i * P + P], kc[:, i * P:i * P + P])
            for i in range(4):
                last = turn(ps[:, 5, i * P:i * P + P], kTA[:, i, 0:P])
            last.then_inc(s["k_turned"], 1)
            pe.wait_ge(s["g_ready"], 1)
            pe.wait_ge(s["tri_ready"], 1)
            g3 = sm[:, 8].rearrange("p (b d h) -> p b d h", b=NB, d=2)
            o3 = ps[:, 6, 0:16].rearrange("p (b d h) -> p b d h", b=NB, d=2)
            for d in range(2):
                MM(o3[:, :, d], tri[:, 1 - d], g3[:, :, d], start=True, stop=True)
            MM(ps[:, 6, 16:32], ones[:, :], sm[:, 8], start=True, stop=True).then_inc(s["gc_turned"], 1)
            def scores(q_blk, kT, k0, bank0, biased):
                if biased:
                    for par in range(2):
                        MM(ps[:, bank0 + par, :], rev[:, :], bias.rearrange("p (a r) n -> p r a n", r=2)[:, par], start=True, stop=False)
                for a in range(4):
                    for par in range(2):
                        rowsl = slice(64 * par, 64 * par + 64)
                        last = MM(ps[:, bank0 + par, a * P:a * P + P], qTA[rowsl, a, q_blk * P:q_blk * P + P],
                                  kT[rowsl, a, k0:k0 + P], start=not biased, stop=not biased or a == 3)
                last.then_inc(s["scores_turned"], 1)
            scores(0, kTA, 0, 0, False)
            pe.wait_ge(s["bias_masked"], 1)
            scores(1, kTA, P, 2, True)
            pe.wait_ge(s["k_saved"], 2)
            scores(1, kcT, 0, 4, False)
            pe.wait_ge(s["grep_ready"], 1)
            pe.wait_ge(s["gc_saved"], 1)
            for b in range(NB):
                if b:
                    pe.wait_ge(s["diff_ready"], b)
                for i in range(8):
                    last = MM(ps[:, 6 + i // 4, (i % 4) * P:(i % 4 + 1) * P], attn[:, 8 * b + i], tri[:, 1 - i // 4], start=True, stop=True)
                last.then_inc(s["gcrow_turned"], 1)
            pe.wait_ge(s["sq_ready"], 1)
            pe.wait_ge(s["diff_ready"], 2)
            for i in range(16):
                last = MM(ps[:, 6, i:i + 1], R[:, i], ones[:, 0:1], start=True, stop=True)
            last.then_inc(s["ss_turned"], 1)
            PR = (X[:, 0:8], X[:, 8:16], XT[:, 0:8])
            PT = (M1[:, 0:8], M1[:, 8:16], XT[:, 8:16])
            pe.wait_ge(s["p_exp"], 3)
            for i in range(3):
                for h in range(8):
                    last = turn(ps[:, 2 * i + h // 4, (h % 4) * P:(h % 4 + 1) * P], PR[i][:, h])
                last.then_inc(s["p_turned"], 1)
            pe.wait_ge(s["len_diag"], 2)
            for i in range(4):
                if i == 2:
                    pe.wait_ge(s["pT_saved"], 3)
                last = MM(ps[:, 4 + (i + 2) % 4, :], ones[:, :], LT[:, 4 * ((i + 2) % 4):4 * ((i + 2) % 4) + 4].rearrange("p a n -> p (a n)"),
                          start=True, stop=True)
            last.then_inc(s["len_turned"], 1)
            for b in range(NB):
                for h in range(H_A):
                    at = 4 * (h % 2) + h // 2
                    cut = slice(h * DH_A, h * DH_A + DH_A)
                    last = MM(ps[:, b, cut], PT[b][:, at], vA[:, b, cut], start=True, stop=b == 0)
                    if b:
                        last = MM(ps[:, b, cut], PT[2][:, at], vc[:, cut], start=False, stop=True)
                last.then_inc(s["o_turned"], 1)
            def tile(i, h, b):
                return b_ch[:, 4 * i + h, b * P:b * P + P]
            pe.wait_ge(s["kn_ready"], 1)
            pe.wait_ge(s["qn_ready"], 1)
            pe.wait_ge(s["oa_ready"], 2)
            for b in range(NB):
                for h in range(H_B):
                    MM(ps[:, b, h * P:h * P + P], tile(1, h, b), tile(1, h, b), start=True, stop=True)
                    last = MM(ps[:, 2 + b, h * P:h * P + P], tile(0, h, b), tile(1, h, b), start=True, stop=True)
                last.then_inc(s["qk_turned"], 1)
            for b in range(NB):
                for h in range(H_B):
                    last = turn(ps[:, 4 + b, h * P:h * P + P], tile(2, h, b))
            last.then_inc(s["v_turned"], 1)
            for h in range(H_B):
                last = turn(ps[:, 6, h * P:h * P + P], tile(1, h, 0))
            last.then_inc(s["ktok_turned"], 1)
            pe.wait_ge(s["ktok_saved"], 1)
            for d in range(2):
                for h in range(H_B):
                    last = MM(ps[:, 6 + d, h * P:h * P + P], tile(1, h, 1), s0[:, d, h], start=True, stop=True)
            last.then_inc(s["ks_turned"], 1)
            pe.wait_ge(s["L_masked"], 2)
            for i in range(16):
                last = turn(ps[:, i // 4, (i % 4) * P:(i % 4 + 1) * P], decay[:, i])
            last.then_inc(s["L_turned"], 1)
            pe.wait_ge(s["attn_masked"], 2)
            pe.wait_ge(s["rhs_ready"], 1)
            for i in range(16):
                last = turn(ps[:, 4 + i // 4, (i % 4) * P:(i % 4 + 1) * P], attn[:, i])
            last.then_inc(s["attn_turned"], 1)
            pe.wait_ge(s["attnT_saved"], 1)
            with pe.Fori(0, (LEVELS - 1) // 2) as r:
                for half in range(2):
                    l = 2 * r + half
                    ct = (CTa, decay)[half]

                    def m1(g):
                        pe.wait_ge(s["xx_saved"], 4 * l + g + 1)
                        if g % 2 == 0:
                            pe.wait_ge(s["ct_ready"], 2 * l + g // 2 + 1)
                        for i in range(4 * g, 4 * g + 4):
                            last = MM(ps[:, g, (i % 4) * P:(i % 4 + 1) * P], ct[:, i], X[:, i], start=True, stop=True)
                        last.then_inc(s["m1_turned"], 1)

                    def xx(g):
                        pe.wait_ge(s["m1_saved"], 4 * l + g + 1)
                        pe.wait_ge(s["xx_saved"], 4 * l + g + 3)
                        for i in range(4 * g, 4 * g + 4):
                            cut = slice((i % 4) * P, (i % 4 + 1) * P)
                            MM(ps[:, 4 + 2 * (g % 2), cut], XT[:, i], M1[:, i], start=True, stop=True)
                            last = MM(ps[:, 5 + 2 * (g % 2), cut], M1[:, i], XT[:, i], start=True, stop=True)
                        last.then_inc(s["xx_turned"], 1)
                    m1(0)
                    m1(1)
                    xx(0)
                    m1(2)
                    xx(1)
                    m1(3)
                    xx(2)
                    xx(3)
            for g in range(4):
                pe.wait_ge(s["xx_saved"], 4 * LEVELS - 4 + g + 1)
                for i in range(4 * g, 4 * g + 4):
                    last = MM(ps[:, g, (i % 4) * P:(i % 4 + 1) * P], XT[:, i], R[:, i], start=True, stop=True)
                last.then_inc(s["vnew_turned"], 1)
            for b in range(NB):
                pe.wait_ge(s["vnew_saved"], 2 * b + 2)
                for h in range(H_B):
                    for d in range(2):
                        i = 8 * b + 4 * d + h
                        last = MM(ps[:, 4 + b, h * P:h * P + P], attn[:, i], M1[:, i], start=d == 0, stop=d == 1)
                last.then_inc(s["o_b_turned"], 1)
            for d in range(2):
                for h in range(H_B):
                    last = MM(ps[:, 6 + d, h * P:h * P + P], tile(0, h, 1), s0[:, d, h], start=True, stop=True)
            last.then_inc(s["qs_turned"], 1)
            pe.wait_ge(s["kd_ready"], 2)
            for i in range(8):
                last = MM(ps[:, i // 4, (i % 4) * P:(i % 4 + 1) * P], CTa[:, i], M1[:, i], start=True, stop=True)
            last.then_inc(s["state_turned"], 1)

            pe.wait_ge(s["yb_ready"], 1)
            pe.wait_ge(s["state_saved"], 1)
            for b in range(NB):
                for t in range(KT):
                    last = turn(ps[:, 2 * b + t // 4, (t % 4) * P:(t % 4 + 1) * P], y[:, b, t * P:t * P + P])
                last.then_inc(s["y_turned"], 1)
            pe.wait_ge(s["yT_lo"], 2)
            for n in range(WOUT, FFN):
                h, cc = (n - WOUT) % 2, (n - WOUT) // 2
                multiply(pe, n, n, hTh1, hTl1, 4 * h, [(0, 4 + cc), (1, 6 + cc)], h == 0, h == 1)

            def gates(i):
                for q in range(4):
                    pe.wait_ge(s["diag_ready"], 4 * i + q + 1)
                    last = MM(ps[:, q, :], ones[:, :], diag[:, q].rearrange("p a n -> p (a n)"), start=True, stop=True)
                last.then_inc(s["gates_turned"], 1)

            gates(0)
            turn_xn(1, 1, xn1)
            pe.wait_ge(s["h_lo_ready"], 4)
            pe.wait_ge(s["gates_saved"], 1)
            pe.wait_ge(s["zr_ready"], 1)
            pe.wait_ge(s["csplit_ready"], 2)

            def ffn_gate_up(n, k, which):
                for i in range(2):
                    multiply(pe, n + 2 * which + i, k + 2 * which + i, hTh1, hTl1, 4 * i,
                             [(b, 2 * b + which) for b in range(NB)], i == 0, i == 1)

            def ffn_down_proj(n, k, stop=False):
                for i in range(2):
                    multiply(pe, n + i, k + i, hcTh, hcTl, 0, [(b, 4 + 2 * b + i) for b in range(NB)], False, stop)

            def ffn_boundary(n, k, c, first=False):
                for b in range(NB):
                    pe.wait_ge(s["h_ready"], NB * c + b + 1)
                    for t in range(4):
                        last = turn(ps[:, 2 * b, t * P:t * P + P], hc[:, b, t * P:t * P + P])
                    last.then_inc(s["h_turned"], 1)
                    if b == 0 and not first:
                        mod_cols(m41, (0, 1), 1)
                mod_product(n, k, csp1, 3)
                if not first:
                    pe.wait_ge(s["mod_cols_saved"], MOD_FFN + c)
                mod_product(n + 2, k + 2, csp1, 1)

            for b in range(NB):
                for h in range(2):
                    MM(ps[:, 4 + 2 * b + h, :], zr[:, 0:P], zr[:, P:P + 512], start=True, stop=False)
            for which in range(2):
                ffn_gate_up(FFN, FFN, which)
            ffn_boundary(FFN + 4, FFN + 4, 0, first=True)
            with pe.Fori(0, (NC - 1) // UNROLL) as r:
                for u in range(UNROLL):
                    k = ffn_unit(u)
                    n = k + FFN_CHUNK * UNROLL * r
                    c = UNROLL * r + u + 1
                    pe.wait_ge(s["hc_lo"], NB * c)
                    ffn_gate_up(n, k, 0)
                    pe.wait_ge(s["mod_rows_copied"], MOD_FFN + 2 * c)
                    ffn_gate_up(n, k, 1)
                    ffn_down_proj(n + 4, k + 4)
                    ffn_boundary(n + 6, k + 6, c)
            pe.wait_ge(s["mod_rows_copied"], 24)
            pe.wait_ge(s["hc_lo"], NB * NC)
            gates(1)
            ffn_down_proj(MOE - 2, MOE - 2, stop=True)
            pe.wait_ge(s["gates_saved"], 2)
            mod_cols(m41, (0, 1), 1)

            pe.wait_ge(s["band_ready"], 1)
            MM(ps[:, 3, :], ones[:, :], flat(band), start=True, stop=True).then_inc(s["counts_turned"], 1)
            pe.wait_ge(s["band_scaled"], 1)
            for b in range(NB):
                pe.wait_ge(s["xn_ready"], 4 + b + 1)
                for t in range(KT):
                    last = MM(ps[:, 2 * b + t // 4, (t % 4) * P:(t % 4 + 1) * P], xn1[:, b, t * P:t * P + P], band[:, t // 2],
                              start=True, stop=True)
                last.then_inc(s["pooled"], 1)
            pe.wait_ge(s["poolw_loaded"], 16)
            for b in range(NB):
                pe.wait_ge(s["yp_ready"], b + 1)
                for g in range(4):
                    for t in range(2):
                        last = MM(ps[:, 4 + 2 * b + g // 2, (g % 2) * 256:(g % 2 + 1) * 256], hTf1[:, 2 * g + t, b * P:b * P + P],
                                  poolw[:, 2 * g + t, :], start=t == 0, stop=t == 1)
            last.then_inc(s["pool_mixed"], 1)
            gates(2)
            turn_xn(2, 3, xn1)
            pe.wait_ge(s["hT_by_vector"], 6)
            pe.wait_ge(s["hT_by_scalar"], 6)
            pe.wait_ge(s["gates_saved"], 3)
            pe.wait_ge(s["poolw_loaded"], 32)
            for b in range(NB):
                for t in range(KT):
                    last = MM(ps[:, 0, 8 * b:8 * b + 8], hTf1[:, t, b * P:b * P + P], w_rt[:, t, :], start=t == 0, stop=t == KT - 1)
            last.then_inc(s["logits_turned"], 1)
            for b in range(NB):
                for t in range(KT):
                    last = turn(ps[:, 4 + 2 * b + t // 4, (t % 4) * P:(t % 4 + 1) * P], hTf1[:, t, b * P:b * P + P])
                last.then_inc(s["htok_turned"], 1)
            pe.wait_ge(s["mask_ready"], 1)
            MM(ps[:, 1, 0:8], sup[:, :], rt[:, 7, 0], start=True, stop=True)
            MM(ps[:, 1, 8:16], ones[:, :], rt[:, 7, 0], start=True, stop=False)
            MM(ps[:, 1, 8:16], sup[:, :], rt[:, 7, 1], start=False, stop=True)
            MM(ps[:, 1, 16:24], ones[:, :], rt[:, 7, 0], start=True, stop=False)
            MM(ps[:, 1, 16:24], ones[:, :], rt[:, 7, 1], start=False, stop=True).then_inc(s["pos_turned"], 1)

            def gather_hi(cnt):
                pe.wait_ge(s["st_ready"], cnt)
                for b in range(NB):
                    turn(ps[:, 5, b * P:b * P + P], ST[:, b].bitcast(F32))
                gather_part(htok_h, "gathered_hi")

            def gather_part(tok, name):
                for t in range(KT):
                    for b in range(NB):
                        last = MM(ps[:, 6 + t // 4, (t % 4) * P:(t % 4 + 1) * P], tok[:, b, t * P:t * P + P], ST[:, b],
                                  start=b == 0, stop=b == 1)
                last.then_inc(s[name], 1)

            def scatter(b):
                for h in range(2):
                    MM(ps[:, 6 + h, :], Sm[:, b], yh[:, 512 * h:512 * h + 512], start=True, stop=False)
                    last = MM(ps[:, 6 + h, :], Sm[:, b], yl[:, 512 * h:512 * h + 512], start=False, stop=True)
                last.then_inc(s["scattered"], 1)

            def expert(n0, hbase, q, j):
                def gate_up(m, start_k, k_from, k_to):
                    for k in range(k_from, k_to):
                        multiply(pe, m + k, start_k + k, hTh1, hTl1, 4 * (k % 2), [(q, k // 2)], k % 2 == 0, k % 2 == 1)

                def down_proj(m, start_k, stop=False):
                    for k in range(2):
                        multiply(pe, m + k, start_k + k, hcTh, hcTl, 0, [(0, 2 + k)], False, stop)

                def turn_hidden(cnt):
                    pe.wait_ge(s["h_ready"], cnt + 1)
                    for t in range(4):
                        last = turn(ps[:, 4, t * P:t * P + P], hc[:, 0, t * P:t * P + P])
                    last.then_inc(s["h_turned"], 1)

                pe.wait_ge(s["xg_hi"], j + 1)
                pe.wait_ge(s["xg_lo"], j + 1)
                gate_up(n0, 0, 0, 4)
                pe.wait_ge(s["y_lo"], j + 1)
                scatter(0)
                for k in range(2):
                    MM(ps[:, 2 + k, :], zr[:, 0:P], zr[:, P:P + 512], start=True, stop=False)
                turn_hidden(hbase)
                for cc in (1, 2):
                    m = n0 + 6 * cc - 2
                    gate_up(m, 4, 0, 2)
                    if cc == 1:
                        pe.wait_ge(s["acc_added"], 2 * j + 1)
                        scatter(1)
                    else:
                        pe.wait_ge(s["xg_hi"], j + 2)
                        gather_part(htok_l, "gathered_lo")
                    gate_up(m, 4, 2, 4)
                    pe.wait_ge(s["hc_lo"], hbase + cc)
                    down_proj(m + 4, 8)
                    turn_hidden(hbase + cc)
                    if cc == 1:
                        pe.wait_ge(s["s_saved"], j + 1)
                        gather_hi(j + 2)
                with pe.Fori(3, NC) as cc:
                    m = n0 + 6 * cc - 2
                    gate_up(m, 4, 0, 4)
                    pe.wait_ge(s["hc_lo"], hbase + cc)
                    down_proj(m + 4, 8)
                    turn_hidden(hbase + cc)
                pe.wait_ge(s["hc_lo"], hbase + NC)
                down_proj(n0 + UNITS_E - 2, 4, stop=True)

            pe.wait_ge(s["npass_ready"], 1)
            passes = nc.tensor.value_load(npass[0:1, 0:1], min_val=1, max_val=2)
            gates(3)
            pe.wait_ge(s["htok_lo"], 2)
            gather_hi(1)
            pe.wait_ge(s["xg_hi"], 1)
            gather_part(htok_l, "gathered_lo")
            pe.wait_ge(s["gates_saved"], 4)
            for k in range(2):
                last = MM(ps[:, 2 + k, :], zr[:, 0:P], zr[:, P:P + 512], start=True, stop=True)
            last.then_inc(s["result_zeroed"], 1)
            with pe.Fori(0, passes) as p:
                with pe.Fori(0, N_EXP // 2) as e2:
                    for q in range(2):
                        j = p * N_EXP + e2 * 2 + q
                        expert(MOE + UNITS_E * j, NB * NC + NC * j, q, j)
            pe.wait_ge(s["y_lo"], passes * N_EXP + 1)
            scatter(0)
            pe.wait_ge(s["acc_added"], passes * (2 * N_EXP) + 1)
            scatter(1)


_INS = ["x_prompt", "x_sample", "cache_k_ctx", "cache_v_ctx", "state_delta", "c", "c_ctx", "w_mod", "b_mod", "norm_g",
        "final_g", "w_in", "conv_w", "a_log", "dt_bias", "rpb", "o_gain", "w_out", "ffn_gate", "ffn_up", "ffn_down",
        "pool_w", "pool_scale", "w_router", "moe_gate", "moe_up", "moe_down"]
_OUTS = [(1, 128, 1024), (1, 128, 1024), (1, 1, 128, 8, 64), (1, 1, 128, 8, 64), (1, 1, 2, 4, 128, 128)]


def kernel(**inputs):
    import numpy as _np
    import concourse.bacc as _bacc
    from concourse import mybir as _mybir
    from concourse.bass_utils import run_bass_kernel_spmd as _run

    nc = _bacc.Bacc("TRN2", target_bir_lowering=False, num_devices=1, dynamic_dma_scratch_size=64)
    arrays, args = {}, []
    for name in _INS:
        a = _np.ascontiguousarray(inputs[name])
        arrays[f"in_{name}"] = a
        args.append(nc.dram_tensor(f"in_{name}", a.shape, _mybir.dt.from_np(a.dtype), kind="ExternalInput").ap())
    for i, shape in enumerate(_OUTS):
        args.append(nc.dram_tensor(f"out_{i}", shape, _mybir.dt.float32, kind="ExternalOutput").ap())
    build(nc, *args)
    r = _run(nc, [arrays], core_ids=[0])
    return tuple(r.results[0][f"out_{i}"] for i in range(len(_OUTS)))
```
